# Optimizing a Trainium2 kernel written in Bass

```python
import jax
import jax.numpy as jnp
from jax import lax
import numpy as np

D_MODEL = 1024
BATCH = 1
SEQ = 1024
DEPTH = 1
DEC_BATCH = 8
DEC_SEQ = 16
PAST_LEN = 1024

CHUNK = 64
GLA_HEADS = 4
GLA_DK = D_MODEL // 2
GLA_DV = D_MODEL
GLA_DK_HEAD = GLA_DK // GLA_HEADS
GLA_DV_HEAD = GLA_DV // GLA_HEADS
GLA_GATE_RANK = 16
GLA_TAU = 16.0
GLA_BLOCK = CHUNK // 4
SB_HEADS = 16
SB_HD = 64
SB_DIM = SB_HEADS * SB_HD
SB_BLOCK = 128
PEER_HEADS = 8
PEER_DK = 256
PEER_HALF = PEER_DK // 2
N_KEYS = 128
N_EXPERTS = N_KEYS * N_KEYS
PEER_TOPK = 16
PEER_BLOCK = 128
N_MOD = 6
DN_ALPHA = (2.0 * DEPTH) ** 0.25
DN_BETA = (8.0 * DEPTH) ** -0.25
LN_EPS = 1e-5
RMS_EPS = 1e-6
SPLIT_SIZES = (GLA_DK, GLA_DK, GLA_DV, GLA_GATE_RANK, GLA_DV, SB_DIM, SB_DIM, SB_DIM, D_MODEL, D_MODEL)
IN_COLS = sum(SPLIT_SIZES)

kernel_name = 'stream_gla_stickbreak_peer'

def layer_norm(x, w=None, b=None):
    xf = x.astype(jnp.float32)
    mu = jnp.mean(xf, axis=-1, keepdims=True)
    var = jnp.mean(jnp.square(xf - mu), axis=-1, keepdims=True)
    y = (xf - mu) * lax.rsqrt(var + LN_EPS)
    if w is not None:
        y = y * w + b
    return y.astype(x.dtype)

def modulate(x, shift, scale):
    return layer_norm(x) * (1.0 + scale[:, None, :]) + shift[:, None, :]

def split_cols(p):
    out = []
    start = 0
    for size in SPLIT_SIZES:
        out.append(p[..., start:start + size])
        start += size
    return out

def gla_recurrence(q, k, v, log_a, s0):
    B, T, H = q.shape[0], q.shape[1], q.shape[2]
    pad = (-T) % GLA_BLOCK

    def blocks(t):
        t = jnp.pad(t.astype(jnp.float32), ((0, 0), (0, pad), (0, 0), (0, 0)))
        return jnp.moveaxis(t.reshape(B, -1, GLA_BLOCK, t.shape[2], t.shape[3]), 1, 0)

    causal = jnp.tril(jnp.ones((GLA_BLOCK, GLA_BLOCK), dtype=bool))

    def step(s, blk):
        qb, kb, vb, lab = blk
        b = jnp.cumsum(lab, axis=1)
        b_last = b[:, -1]
        qe = qb * jnp.exp(b)
        ke = kb * jnp.exp(-b)
        kd = kb * jnp.exp(b_last[:, None] - b)
        att = jnp.where(causal[None, None], jnp.einsum('blhk,bmhk->bhlm', qe, ke), 0.0)
        o = jnp.einsum('blhk,bhkv->blhv', qe, s) + jnp.einsum('bhlm,bmhv->blhv', att, vb)
        s_new = jnp.exp(b_last)[..., None] * s + jnp.einsum('blhk,blhv->bhkv', kd, vb)
        return s_new, o

    s_fin, o = lax.scan(step, s0.astype(jnp.float32), (blocks(q), blocks(k), blocks(v), blocks(log_a)))
    o = jnp.moveaxis(o, 0, 1).reshape(B, T + pad, H, v.shape[3])[:, :T]
    return o, s_fin

def stick_breaking(q, k, v, q_pos, k_pos):
    z = jnp.einsum('bqhd,bkhd->bhqk', q, k).astype(jnp.float32) * (SB_HD ** -0.5)
    mask = k_pos[None, :] < q_pos[:, None]
    log_rest = jnp.where(mask, jax.nn.log_sigmoid(-z), 0.0)
    after = lax.cumsum(log_rest, axis=3, reverse=True) - log_rest
    a = jnp.where(mask, jnp.exp(jax.nn.log_sigmoid(z) + after), 0.0)
    return jnp.einsum('bhqk,bkhd->bqhd', a.astype(v.dtype), v)

def peer_block(h, peer_wq, peer_keys, peer_u, peer_v):
    n = h.shape[0]
    q = (h @ peer_wq).reshape(n, PEER_HEADS, 2, PEER_HALF)
    s = jnp.einsum('nhpd,hpkd->nhpk', q, peer_keys).astype(jnp.float32)
    sc, ix = lax.top_k(s, PEER_TOPK)
    cand = (sc[:, :, 0, :, None] + sc[:, :, 1, None, :]).reshape(n, PEER_HEADS, PEER_TOPK * PEER_TOPK)
    cid = (ix[:, :, 0, :, None] * N_KEYS + ix[:, :, 1, None, :]).reshape(n, PEER_HEADS, PEER_TOPK * PEER_TOPK)
    top, pos = lax.top_k(cand, PEER_TOPK)
    eid = jnp.take_along_axis(cid, pos, axis=-1)
    g = jax.nn.softmax(top, axis=-1)
    act = jax.nn.gelu(jnp.einsum('nhkd,nd->nhk', peer_u[eid], h).astype(jnp.float32))
    w = (g * act).astype(h.dtype)
    return jnp.einsum('nhk,nhkd->nd', w, peer_v[eid])

def peer(h, peer_wq, peer_keys, peer_u, peer_v):
    B, T, D = h.shape
    n = B * T
    pad = (-n) % PEER_BLOCK
    hb = jnp.pad(h.reshape(n, D), ((0, pad), (0, 0))).reshape(-1, PEER_BLOCK, D)
    out = lax.map(lambda blk: peer_block(blk, peer_wq, peer_keys, peer_u, peer_v), hb)
    return out.reshape(-1, D)[:n].reshape(B, T, D)

def trunk_layer(x, c, gla_s0, k_past, v_past, w_ada, b_ada, w_in, w_gla_gate, b_gla_gate, gla_norm_w,
                w_gla_proj, w_sb_proj, w_o, ln1_w, ln1_b, peer_wq, peer_keys, peer_u, peer_v, ln2_w, ln2_b):
    B, T, _ = x.shape
    mod = jax.nn.silu(c) @ w_ada + b_ada
    sh1, sc1, g1, sh2, sc2, g2 = jnp.split(mod, N_MOD, axis=-1)

    h = modulate(x, sh1, sc1)
    gq, gk, gv, glr, gog, sq, sk, sv, mg_a, mg_b = split_cols(h @ w_in)

    q = gq.reshape(B, T, GLA_HEADS, GLA_DK_HEAD) * (GLA_DK_HEAD ** -0.5)
    k = gk.reshape(B, T, GLA_HEADS, GLA_DK_HEAD)
    v = gv.reshape(B, T, GLA_HEADS, GLA_DV_HEAD)
    log_a = (jax.nn.log_sigmoid((glr @ w_gla_gate + b_gla_gate).astype(jnp.float32)) / GLA_TAU
             ).reshape(B, T, GLA_HEADS, GLA_DK_HEAD)
    if gla_s0 is None:
        gla_s0 = jnp.zeros((B, GLA_HEADS, GLA_DK_HEAD, GLA_DV_HEAD), jnp.float32)
    o_gla, s_fin = gla_recurrence(q, k, v, log_a, gla_s0)
    o_gla = o_gla * lax.rsqrt(jnp.mean(jnp.square(o_gla), axis=-1, keepdims=True) + RMS_EPS) * gla_norm_w
    o_gla = o_gla.reshape(B, T, GLA_DV).astype(x.dtype) * jax.nn.silu(gog)
    branch_a = o_gla @ w_gla_proj

    sbq = sq.reshape(B, T, SB_HEADS, SB_HD)
    sbk = sk.reshape(B, T, SB_HEADS, SB_HD)
    sbv = sv.reshape(B, T, SB_HEADS, SB_HD)
    if k_past is None:
        outs = []
        for i in range(T // SB_BLOCK):
            lo, hi = i * SB_BLOCK, (i + 1) * SB_BLOCK
            outs.append(stick_breaking(sbq[:, lo:hi], sbk[:, :hi], sbv[:, :hi], jnp.arange(lo, hi), jnp.arange(hi)))
        o_sb = jnp.concatenate(outs, axis=1)
    else:
        past = k_past.shape[1]
        k_all = jnp.concatenate([k_past, sbk], axis=1)
        v_all = jnp.concatenate([v_past, sbv], axis=1)
        o_sb = stick_breaking(sbq, k_all, v_all, past + jnp.arange(T), jnp.arange(past + T))
    branch_b = o_sb.reshape(B, T, SB_DIM) @ w_sb_proj

    mix = (jax.nn.sigmoid(mg_a) * branch_a + jax.nn.sigmoid(mg_b) * branch_b) @ w_o
    x = layer_norm(DN_ALPHA * x + g1[:, None, :] * mix, ln1_w, ln1_b)

    h2 = modulate(x, sh2, sc2)
    f = peer(h2, peer_wq, peer_keys, peer_u, peer_v)
    x = layer_norm(DN_ALPHA * x + g2[:, None, :] * f, ln2_w, ln2_b)
    return x, s_fin.astype(x.dtype), sbk, sbv

def setup_inputs(seed: int = 0) -> dict:
    key = jax.random.key(seed)
    ks = jax.random.split(key, 26)

    def nrm(k, shape, scale):
        return jax.random.normal(k, shape, jnp.float32) * scale

    D = D_MODEL
    return {
        'x_prompt': nrm(ks[0], (BATCH, SEQ, D), 1.0),
        'x_sample': nrm(ks[1], (DEC_BATCH, DEC_SEQ, D), 1.0),
        'state_gla': nrm(ks[2], (DEPTH, DEC_BATCH, GLA_HEADS, GLA_DK_HEAD, GLA_DV_HEAD), 0.5),
        'cache_sb_k': nrm(ks[3], (DEPTH, DEC_BATCH, PAST_LEN, SB_HEADS, SB_HD), 1.0),
        'cache_sb_v': nrm(ks[4], (DEPTH, DEC_BATCH, PAST_LEN, SB_HEADS, SB_HD), 1.0),
        'c_prompt': nrm(ks[5], (BATCH, D), 1.0),
        'c_sample': nrm(ks[6], (DEC_BATCH, D), 1.0),
        'w_ada': nrm(ks[7], (DEPTH, D, N_MOD * D), D ** -0.5),
        'b_ada': nrm(ks[8], (DEPTH, N_MOD * D), 0.02),
        'w_in': nrm(ks[9], (DEPTH, D, IN_COLS), D ** -0.5),
        'w_gla_gate': nrm(ks[10], (DEPTH, GLA_GATE_RANK, GLA_DK), GLA_GATE_RANK ** -0.5),
        'b_gla_gate': nrm(ks[11], (DEPTH, GLA_DK), 0.1),
        'gla_norm_w': 1.0 + nrm(ks[12], (DEPTH, GLA_DV_HEAD), 0.02),
        'w_gla_proj': nrm(ks[13], (DEPTH, GLA_DV, D), DN_BETA * GLA_DV ** -0.5),
        'w_sb_proj': nrm(ks[14], (DEPTH, SB_DIM, D), DN_BETA * SB_DIM ** -0.5),
        'w_o': nrm(ks[15], (DEPTH, D, D), DN_BETA * D ** -0.5),
        'ln1_w': 1.0 + nrm(ks[16], (DEPTH, D), 0.02),
        'ln1_b': nrm(ks[17], (DEPTH, D), 0.02),
        'peer_wq': nrm(ks[18], (DEPTH, D, PEER_HEADS * PEER_DK), D ** -0.5),
        'peer_keys': nrm(ks[19], (DEPTH, PEER_HEADS, 2, N_KEYS, PEER_HALF), PEER_HALF ** -0.5),
        'peer_u': nrm(ks[20], (DEPTH, N_EXPERTS, D), D ** -0.5),
        'peer_v': nrm(ks[21], (DEPTH, N_EXPERTS, D), DN_BETA),
        'ln2_w': 1.0 + nrm(ks[22], (DEPTH, D), 0.02),
        'ln2_b': nrm(ks[23], (DEPTH, D), 0.02),
    }

def reference(x_prompt, x_sample, state_gla, cache_sb_k, cache_sb_v, c_prompt, c_sample,
              w_ada, b_ada, w_in, w_gla_gate, b_gla_gate, gla_norm_w, w_gla_proj, w_sb_proj, w_o,
              ln1_w, ln1_b, peer_wq, peer_keys, peer_u, peer_v, ln2_w, ln2_b):
    yp = x_prompt
    ys = x_sample
    sp_list, kp_list, vp_list, ss_list, ksl, vsl = [], [], [], [], [], []
    for l in range(DEPTH):
        params = (w_ada[l], b_ada[l], w_in[l], w_gla_gate[l], b_gla_gate[l], gla_norm_w[l], w_gla_proj[l],
                  w_sb_proj[l], w_o[l], ln1_w[l], ln1_b[l], peer_wq[l], peer_keys[l], peer_u[l], peer_v[l],
                  ln2_w[l], ln2_b[l])
        yp, sp, kp, vp = trunk_layer(yp, c_prompt, None, None, None, *params)
        ys, ss, kss, vss = trunk_layer(ys, c_sample, state_gla[l], cache_sb_k[l], cache_sb_v[l], *params)
        sp_list.append(sp)
        kp_list.append(kp)
        vp_list.append(vp)
        ss_list.append(ss)
        ksl.append(kss)
        vsl.append(vss)
    new_state_gla_prompt = jnp.stack(sp_list, axis=0)
    new_sb_k_prompt = jnp.stack(kp_list, axis=0)
    new_sb_v_prompt = jnp.stack(vp_list, axis=0)
    new_state_gla_sample = jnp.stack(ss_list, axis=0)
    new_sb_k_sample = jnp.stack(ksl, axis=0)
    new_sb_v_sample = jnp.stack(vsl, axis=0)
    return (yp, ys, new_state_gla_prompt, new_sb_k_prompt, new_sb_v_prompt,
            new_state_gla_sample, new_sb_k_sample, new_sb_v_sample)


_drawn_inputs = setup_inputs


def setup_inputs(seed=0):
    import zlib

    import numpy as np

    out = dict(_drawn_inputs(seed))
    spreads = {}
    factors = {'cache_sb_k': 8.895, 'gla_norm_w': 17.311, 'ln2_w': 21.847, 'ln2_b': 23.032}
    for name, (base, spread) in spreads.items():
        noise = np.random.default_rng([zlib.crc32(name.encode()), seed]).standard_normal(out[name].shape)
        drawn = base * np.exp(spread * noise) if base else spread * noise
        out[name] = jnp.asarray(drawn.astype(out[name].dtype))
    for name, factor in factors.items():
        out[name] = (out[name] * factor).astype(out[name].dtype)
    return out
```

```python
from contextlib import ExitStack

import concourse.bass as bass
from concourse import mybir

F32 = mybir.dt.float32
BF16 = mybir.dt.bfloat16
U32 = mybir.dt.uint32
ALU = mybir.AluOpType
ACT = mybir.ActivationFunctionType
AX_X = mybir.AxisListType.X

P = 128
D = 1024
KC = D // P
PROMPT = 1024
SEQS, NEW = 8, 16
TOK = PROMPT + SEQS * NEW
TILES = TOK // P
PTILES = PROMPT // P
PAST = 1024
PBLK = PAST // P
HALF = 512
MODS = 6 * D
SB_PAIRS, HD = 8, 64
GLA_HEADS, DK, DV = 4, 128, 256
SUB = 16
SUBS = P // SUB
RANK = 16
PEER_HEADS, NKEYS, TOPK = 8, 128, 16
CHUNK = 384
CHUNKS = TOK // CHUNK
LN_EPS, RMS_EPS = 1e-5, 1e-6
ALPHA = 2.0 ** 0.25
TAU = 16.0
NEG = -3.0e38


class Scope:

    def __init__(self, nc, ctx, tag):
        self.nc, self.ctx, self.tag, self.sems = nc, ctx, tag, []

    def sb(self, name, shape, dt=F32):
        return self.ctx.enter_context(self.nc.sbuf_tensor(f"{self.tag}_{name}", shape, dt))

    def ps(self, name, shape, dt=F32):
        return self.ctx.enter_context(self.nc.psum_tensor(f"{self.tag}_{name}", shape, dt))

    def sem(self, name):
        s = self.ctx.enter_context(self.nc.semaphore(f"{self.tag}_{name}"))
        self.sems.append(s)
        return s

    def rest(self):
        nums = sorted(s.num for s in self.sems)
        assert nums == list(range(nums[0], nums[-1] + 1))
        self.nc.all_engine_barrier(sems_to_clear=range(nums[0], nums[-1] + 1))


def layer_norm_steps(e, done, inverse, turn, n, x, stats, mv, rstd, out):
    for c in range(2):
        e.bn_stats(stats[:, c, :], x[:, c * HALF:(c + 1) * HALF]).then_inc(done, 1)
    e.wait_ge(done, n + 2)
    e.bn_aggr(mv, stats).then_inc(done, 1)
    e.wait_ge(done, n + 3)
    e.tensor_scalar(rstd, mv[:, 1:2], LN_EPS, None, ALU.add).then_inc(done, 1)
    e.wait_ge(done, n + 4)
    e.reciprocal(rstd, rstd).then_inc(done, 1)
    e.wait_ge(inverse, turn + 1)
    e.tensor_scalar(out, x, mv[:, 0:1], rstd, ALU.subtract, ALU.mult).then_inc(done, 1)
    return n + 6


def mods_phase(nc, A, modb):
    BLK = MODS // HALF
    RING = 3
    with ExitStack() as ctx:
        S = Scope(nc, ctx, "mod")
        c_sb, silu_c = S.sb("c", [P, KC * (1 + SEQS)]), S.sb("silu", [P, KC * (1 + SEQS)])
        bias, ones = S.sb("bias", [1, MODS]), S.sb("ones", [1, 1 + SEQS])
        sel = S.sb("sel", [1 + SEQS, 2, P])
        w = S.sb("w", [P, RING, KC, HALF])
        mod = S.sb("mod", [1 + SEQS, MODS])
        spread = S.sb("spread", [P, 2, MODS])
        acc = [S.ps(f"acc{i}", [1 + SEQS, HALF]) for i in range(2)]
        rows = [S.ps(f"rows{i}", [P, HALF]) for i in range(2)]
        small_in, bias_in, sel_in = S.sem("small_in"), S.sem("bias_in"), S.sem("sel_in")
        w_in = [S.sem(f"w_in{i}") for i in range(RING)]
        ones_set, silu_done, acc_full, mod_kept = S.sem("ones"), S.sem("silu"), S.sem("acc_full"), S.sem("mod_kept")
        rows_full, rows_kept, stored = S.sem("rows_full"), S.sem("rows_kept"), S.sem("stored")
        with nc.Block() as block:

            @block.sync
            def _(sp):
                sp.dma_start(c_sb[:, :], A["cT"]).then_inc(small_in, 16)
                for j in range(BLK):
                    if j >= RING:
                        sp.wait_ge(acc_full, j - RING + 1)
                    sp.dma_start(w[:, j % RING], A["w_ada"].rearrange("(k p) n -> p k n", p=P)[:, :, j * HALF:(j + 1) * HALF]).then_inc(w_in[j % RING], 16)
                sp.wait_ge(rows_kept, 2 * BLK)
                sp.dma_start(modb.rearrange("g p n -> p g n"), spread[:, :, :]).then_inc(stored, 16)
                sp.wait_ge(stored, 16)

            @block.scalar
            def _(act):
                act.dma_start(bias[:, :], A["b_ada"]).then_inc(bias_in, 16)
                act.dma_start(sel[:, :, :], A["sel"]).then_inc(sel_in, 16)
                act.wait_ge(small_in, 16)
                act.activation(silu_c[:, :], c_sb[:, :], ACT.Silu).then_inc(silu_done, 1)
                for n in range(2 * BLK):
                    j, g = n // 2, n % 2
                    act.wait_ge(rows_full, n + 1)
                    act.activation(spread[:, g, j * HALF:(j + 1) * HALF], rows[n % 2][:, :], ACT.Copy).then_inc(rows_kept, 1)

            @block.tensor
            def _(pe):
                pe.wait_ge(silu_done, 1)
                pe.wait_ge(bias_in, 16)
                pe.wait_ge(ones_set, 1)
                for j in range(BLK):
                    if j >= 2:
                        pe.wait_ge(mod_kept, j - 1)
                    pe.wait_ge(w_in[j % RING], 16 * (j // RING + 1))
                    for k in range(KC):
                        pe.matmul(acc[j % 2][:, :], silu_c[:, k * (1 + SEQS):(k + 1) * (1 + SEQS)], w[:, j % RING, k, :], start=(k == 0), stop=False)
                    pe.matmul(acc[j % 2][:, :], ones[0:1, :], bias[0:1, j * HALF:(j + 1) * HALF], start=False, stop=True).then_inc(acc_full, 1)
                pe.wait_ge(sel_in, 16)
                for n in range(2 * BLK):
                    j, g = n // 2, n % 2
                    pe.wait_ge(mod_kept, j + 1)
                    if n >= 2:
                        pe.wait_ge(rows_kept, n - 1)
                    pe.matmul(rows[n % 2][:, :], sel[:, g, :], mod[:, j * HALF:(j + 1) * HALF], start=True, stop=True).then_inc(rows_full, 1)

            @block.vector
            def _(dve):
                dve.memset(ones[:, :], 1.0).then_inc(ones_set, 1)
                for j in range(BLK):
                    dve.wait_ge(acc_full, j + 1)
                    dve.tensor_copy(mod[:, j * HALF:(j + 1) * HALF], acc[j % 2][:, :]).then_inc(mod_kept, 1)
        S.rest()


def norm_phase(nc, A, modb, hT):
    U = 3
    with ExitStack() as ctx:
        S = Scope(nc, ctx, "norm")
        ident = S.sb("ident", [P, P])
        x = S.sb("x", [P, U, D])
        xn = S.sb("xn", [P, U, D])
        h = S.sb("h", [P, U, D])
        mods = S.sb("mods", [P, 2, 2 * D])
        stats, mv, rstd = S.sb("stats", [P, U, 2, 6]), S.sb("mv", [P, U, 2]), S.sb("rstd", [P, U])
        turned = [S.ps(f"turned{i}", [P, 4, P]) for i in range(2)]
        ident_in, x_in, mods_in = S.sem("ident_in"), [S.sem(f"x_in{u}") for u in range(U)], [S.sem(f"mods_in{g}") for g in range(2)]
        inverse = S.sem("inverse")
        normed, h_ready, turned_full, hT_kept = S.sem("normed"), S.sem("h_ready"), S.sem("turned_full"), S.sem("hT_kept")
        with nc.Fori(0, TILES // U) as i:
            with nc.Block() as block:

                @block.sync
                def _(sp):
                    for u in range(U):
                        sp.dma_start(x[:, u, :], A["x"].rearrange("(t p) n -> t p n", p=P)[U * i + u]).then_inc(x_in[u], 16)
                    sp.dma_start(ident[:, :], A["ident"]).then_inc(ident_in, 16)

                @block.scalar
                def _(act):
                    act.dma_start(mods[:, 0, :], modb[0, :, 0:2 * D]).then_inc(mods_in[0], 16)
                    act.dma_start(mods[:, 1, :], modb[i // 2, :, 0:2 * D]).then_inc(mods_in[1], 16)
                    for u in range(U):
                        act.wait_ge(normed, 6 * u + 5)
                        act.activation(rstd[:, u:u + 1], rstd[:, u:u + 1], ACT.Sqrt).then_inc(inverse, 1)
                    for n in range(2 * U):
                        u, c = n // 2, n % 2
                        act.wait_ge(turned_full, n + 1)
                        act.activation(hT[:, 4 * c:4 * c + 4, bass.ds(U * P * i + P * u, P)], turned[n % 2][:, :, :], ACT.Copy).then_inc(hT_kept, 1)

                @block.tensor
                def _(pe):
                    pe.wait_ge(ident_in, 16)
                    for n in range(2 * U):
                        u, c = n // 2, n % 2
                        pe.wait_ge(h_ready, 2 * u + 2)
                        if n >= 2:
                            pe.wait_ge(hT_kept, n - 1)
                        for k in range(4):
                            last = pe.transpose(turned[n % 2][:, k, :], h[:, u, (4 * c + k) * P:(4 * c + k + 1) * P], ident[:, :])
                        last.then_inc(turned_full, 1)

                @block.vector
                def _(dve):
                    n = 0
                    for u in range(U):
                        dve.wait_ge(x_in[u], 16)
                        n = layer_norm_steps(dve, normed, inverse, u, n, x[:, u, :], stats[:, u], mv[:, u], rstd[:, u:u + 1], xn[:, u, :])
                        dve.wait_ge(normed, n)
                        dve.wait_ge(mods_in[u // 2], 16)
                        m = mods[:, u // 2, :]
                        dve.scalar_tensor_tensor(h[:, u, :], m[:, D:2 * D], 1.0, xn[:, u, :], ALU.add, ALU.mult).then_inc(h_ready, 1)
                        dve.wait_ge(h_ready, 2 * u + 1)
                        dve.tensor_tensor(h[:, u, :], h[:, u, :], m[:, 0:D], ALU.add).then_inc(h_ready, 1)
            S.rest()


def stick_phase(nc, A, hT, oB_dram, kout, vout):
    SC = SEQS * 2 * NEW
    with ExitStack() as ctx:
        S = Scope(nc, ctx, "sb")
        ident, identb = S.sb("ident", [P, P]), S.sb("identb", [P, P], BF16)
        from_here, before = S.sb("from_here", [P, P]), S.sb("before", [P, P])
        hide_diag, hide_self = S.sb("hide_diag", [P, P], BF16), S.sb("hide_self", [P, SC], BF16)
        w = S.sb("w", [P, 3, KC, P])
        qT, kT = S.sb("qT", [P, TOK]), S.sb("kT", [P, TOK])
        v, kn = S.sb("v", [P, TILES, P]), S.sb("kn", [P, TILES, P])
        kc, vc = S.sb("kc", [P, SEQS, PAST]), S.sb("vc", [P, SEQS, PBLK, P])
        qd = S.sb("qd", [P, SEQS, 2, NEW])
        oB = S.sb("oB", [P, TOK])
        NZ, NA = 4, 3
        zs, t, sp_, a = S.sb("zs", [P, NZ, HALF]), S.sb("t", [P, NZ, HALF]), S.sb("sp", [P, NZ, HALF]), S.sb("a", [P, NA, HALF])
        banks = [S.ps(f"bank{i}", [P, HALF]) for i in range(8)]
        zb = banks[0:2]
        rest = dict(X=banks[2], Y=banks[3], C=banks[4])
        o_late, o_early, o_new = banks[5], banks[6], banks[7]

        const_in, w_in = S.sem("const_in"), S.sem("w_in")
        zeros_set = S.sem("zeros_set")
        kc_in, vc_in = S.sem("kc_in"), S.sem("vc_in")
        proj_full, q_kept, k_kept, v_kept, kn_kept, qd_set = (S.sem(n) for n in ("proj_full", "q_kept", "k_kept", "v_kept", "kn_kept", "qd_set"))
        kn_full = S.sem("kn_full")
        z_full, z_kept, t_capped, t_exp, t_log, sp_ready = (S.sem(n) for n in ("z_full", "z_kept", "t_capped", "t_exp", "t_log", "sp_ready"))
        rest_full, e_ready, a_ready, rest_added, o_added = (S.sem(n) for n in ("rest_full", "e_ready", "a_ready", "rest_added", "o_added"))
        o_kept, stored = S.sem("o_kept"), S.sem("stored")

        with nc.Block() as block:

            @block.sync
            def _(sp):
                sp.dma_start(ident[:, :], A["ident"]).then_inc(const_in, 16)
                sp.dma_start(from_here[:, :], A["from_here"]).then_inc(const_in, 16)
                sp.dma_start(before[:, :], A["before"]).then_inc(const_in, 16)
                sp.dma_start(w[:, :, :, :], A["w_sb"][0]).then_inc(w_in, 16)
                sp.wait_ge(w_in, 16)
                sp.wait_ge(const_in, 16 * 5)

            @block.scalar
            def _(act):
                act.dma_start(t[:, 0, 0:P], A["hide_diag"]).then_inc(const_in, 16)
                act.dma_start(t[:, 1, 0:SC], A["hide_self"]).then_inc(const_in, 16)

            @block.vector
            def _(dve):
                dve.memset(qd[:, :, :, :], 0.0).then_inc(zeros_set, 1)
                dve.wait_ge(const_in, 16 * 5)
                dve.tensor_copy(identb[:, :], ident[:, :]).then_inc(zeros_set, 1)
                dve.tensor_copy(hide_diag[:, :], t[:, 0, 0:P]).then_inc(zeros_set, 1)
                dve.tensor_copy(hide_self[:, :], t[:, 1, 0:SC]).then_inc(zeros_set, 1)
                dve.wait_ge(zeros_set, 4)
        S.rest()

        X = [("X", 0, g, kb) for g in (1, 0) for kb in range(4 * g + 3, -1, -1)]
        Y = [("Y", 1, g, kb) for g in (1, 0) for kb in range(4 * g + 3, -1, -1)]
        C = [("C", None, None, kb) for kb in [None] + list(range(PBLK - 1, -1, -1))]
        steps = []
        for n in range(max(len(X), len(C))):
            steps += [c[n] for c in (X, Y, C) if n < len(c)]
        N = len(steps)

        def first_col(step):
            _, head, g, kb = step
            return 0 if head is None else max(0, kb - 4 * g) * P

        def width(step):
            return SC if step[1] is None else HALF

        def chain_start(step):
            _, head, g, kb = step
            return kb is None if head is None else kb == 4 * g + 3

        def last_step(chain, g=None):
            return max(n for n, s in enumerate(steps) if s[0] == chain and s[2] == g) + 1

        late_whole = max(last_step("X", 1), last_step("Y", 1))
        early_whole = max(last_step("X", 0), last_step("Y", 0))
        new_whole = last_step("C")

        with nc.Fori(0, SB_PAIRS) as pair:
            with nc.Block() as block:

                @block.sync
                def _(sp):
                    sp.dma_start(kc[:, :, :], A["kcT"][pair]).then_inc(kc_in, 16)
                    sp.dma_start(vc[:, :, :, :], A["vc"][pair]).then_inc(vc_in, 16)
                    sp.wait_ge(proj_full, 9)
                    sp.dma_start(w[:, :, :, :], A["w_sb"][pair + 1]).then_inc(w_in, 16)
                    sp.wait_ge(kn_kept, 3)
                    sp.dma_start(kout.rearrange("(t p) n -> p t n", p=P)[:, :, bass.ds(pair * P, P)], kn[:, :, :]).then_inc(stored, 16)
                    sp.wait_ge(v_kept, 3)
                    sp.dma_start(vout.rearrange("(t p) n -> p t n", p=P)[:, :, bass.ds(pair * P, P)], v[:, :, :]).then_inc(stored, 16)
                    sp.wait_ge(o_kept, 4)
                    sp.dma_start(oB_dram[pair], oB[:, :]).then_inc(stored, 16)
                    sp.wait_ge(w_in, 16)
                    sp.wait_ge(stored, 48)

                @block.tensor
                def _(pe):
                    for g in range(9):
                        bank = banks[g % 8]
                        if g == 8:
                            pe.wait_ge(q_kept, 1)
                        if g < 6:
                            c = g % 3
                            for k in range(KC):
                                last = pe.matmul(bank[:, 0:CHUNK], w[:, g // 3, k, :], hT[:, k, c * CHUNK:(c + 1) * CHUNK], start=(k == 0), stop=(k == KC - 1))
                        else:
                            for u in range(3):
                                tile = 3 * (g - 6) + u
                                for k in range(KC):
                                    last = pe.matmul(bank[:, u * P:(u + 1) * P], hT[:, k, tile * P:(tile + 1) * P], w[:, 2, k, :], start=(k == 0), stop=(k == KC - 1))
                        last.then_inc(proj_full, 1)
                    for g in range(3):
                        pe.wait_ge(k_kept, g + 1)
                        pe.wait_ge(q_kept, 3)
                        pe.wait_ge(v_kept, 3)
                        for u in range(3):
                            tile = 3 * g + u
                            last = pe.transpose(banks[1 + g][:, u * P:(u + 1) * P], kT[:, tile * P:(tile + 1) * P], ident[:, :])
                        last.then_inc(kn_full, 1)
                    pe.wait_ge(kn_kept, 3)
                    pe.wait_ge(qd_set, 2)

                    def scores(n):
                        step = steps[n]
                        _, head, g, kb = step
                        if n >= 2:
                            pe.wait_ge(z_kept, n - 1)
                        out = zb[n % 2]
                        if head is None and kb is None:
                            pe.matmul(out[:, 0:SC], kT[:, PROMPT:TOK], qd[:, :, :, :].rearrange("p s h t -> p (s h t)"), start=True, stop=False)
                            last = pe.matmul(out[:, 0:SC], identb[:, :], hide_self[:, :], start=False, stop=True)
                        elif head is None:
                            if kb == PBLK - 1:
                                pe.wait_ge(kc_in, 16)
                            for s in range(SEQS):
                                last = pe.matmul(out[:, s * 2 * NEW:(s + 1) * 2 * NEW], kc[:, s, kb * P:(kb + 1) * P],
                                                 qd[:, s].rearrange("p h t -> p (h t)"), start=True, stop=True)
                        else:
                            lo, c0 = head * HD, first_col(step)
                            diagonal = kb >= 4 * g
                            last = pe.matmul(out[:, c0:HALF], kT[lo:lo + HD, kb * P:(kb + 1) * P], qT[lo:lo + HD, g * HALF + c0:(g + 1) * HALF],
                                             start=True, stop=not diagonal)
                            if diagonal:
                                last = pe.matmul(out[:, c0:c0 + P], identb[:, :], hide_diag[:, :], start=False, stop=True)
                        last.then_inc(z_full, 1)

                    def to_here(n):
                        step = steps[n]
                        chain, head, g, kb = step
                        bank = rest[chain]
                        c0, c1 = first_col(step), width(step)
                        pe.wait_ge(sp_ready, n + 1)
                        pe.matmul(bank[:, c0:c1], from_here[:, :], sp_[:, n % NZ, c0:c1], start=chain_start(step), stop=True, skip_group_check=True).then_inc(rest_full, 1)

                    def later_keys(n):
                        step = steps[n]
                        c0, c1 = first_col(step), width(step)
                        pe.wait_ge(e_ready, n + 1)
                        pe.matmul(rest[step[0]][:, c0:c1], before[:, :], sp_[:, n % NZ, c0:c1], start=False, stop=True, skip_group_check=True).then_inc(rest_added, 1)

                    def values(n):
                        step = steps[n]
                        chain, head, g, kb = step
                        c0, c1 = first_col(step), width(step)
                        pe.wait_ge(a_ready, n + 1)
                        if head is None:
                            if kb is None:
                                last = pe.matmul(o_new[:, 0:SC], v[:, TILES - 1, :], a[:, n % NA, 0:SC], start=True, stop=False)
                            else:
                                if kb == PBLK - 1:
                                    pe.wait_ge(vc_in, 16)
                                for s in range(SEQS):
                                    cols = slice(s * 2 * NEW, (s + 1) * 2 * NEW)
                                    last = pe.matmul(o_new[:, cols], vc[:, s, kb, :], a[:, n % NA, cols], start=False, stop=(kb == 0 and s == SEQS - 1))
                        else:
                            out = (o_late if g == 1 else o_early)[head * HD:(head + 1) * HD, :]
                            last = pe.matmul(out[:, c0:HALF], v[:, kb, head * HD:(head + 1) * HD], a[:, n % NA, c0:HALF], start=chain_start(step), stop=(kb == 0), skip_group_check=True)
                        last.then_inc(o_added, 1)

                    for s in range(N + 4):
                        if s < N:
                            scores(s)
                        if 0 <= s - 2 < N:
                            to_here(s - 2)
                        if 0 <= s - 3 < N:
                            later_keys(s - 3)
                        if 0 <= s - 4 < N:
                            values(s - 4)

                @block.scalar
                def _(act):
                    act.preload_act_table_set("natural_log_exp_and_others")
                    for c in range(3):
                        act.wait_ge(proj_full, c + 1)
                        act.activation(qT[:, c * CHUNK:(c + 1) * CHUNK], banks[c][:, 0:CHUNK], ACT.Copy, scale=HD ** -0.5).then_inc(q_kept, 1)
                    act.wait_ge(q_kept, 3)
                    for hh in range(2):
                        rows = slice(hh * HD, (hh + 1) * HD)
                        act.activation(qd[rows, :, hh, :], qT[rows, PROMPT:TOK].rearrange("p (s t) -> p s t", t=NEW), ACT.Copy).then_inc(qd_set, 1)
                    for g in range(3):
                        act.wait_ge(proj_full, 7 + g)
                        act.activation(v[:, 3 * g:3 * g + 3, :].rearrange("p t n -> p (t n)"), banks[(6 + g) % 8][:, 0:CHUNK], ACT.Copy).then_inc(v_kept, 1)

                    def keep(n):
                        c0, c1 = first_col(steps[n]), width(steps[n])
                        act.wait_ge(z_full, n + 1)
                        if n >= NZ:
                            act.wait_ge(a_ready, n - NZ + 1)
                        act.activation(zs[:, n % NZ, c0:c1], zb[n % 2][:, c0:c1], ACT.Copy).then_inc(z_kept, 1)

                    def exp_log(n):
                        c0, c1 = first_col(steps[n]), width(steps[n])
                        act.wait_ge(t_capped, n + 1)
                        act.activation(t[:, n % NZ, c0:c1], t[:, n % NZ, c0:c1], ACT.Exp).then_inc(t_exp, 1)
                        act.wait_ge(t_exp, n + 1)
                        act.activation(t[:, n % NZ, c0:c1], t[:, n % NZ, c0:c1], ACT.Ln, bias=1.0).then_inc(t_log, 1)

                    def weights(n):
                        c0, c1 = first_col(steps[n]), width(steps[n])
                        act.wait_ge(e_ready, n + 1)
                        if n >= NA:
                            act.wait_ge(o_added, n - NA + 1)
                        act.activation(a[:, n % NA, c0:c1], zs[:, n % NZ, c0:c1], ACT.Exp).then_inc(a_ready, 1)

                    for s in range(N + 3):
                        if s < N:
                            keep(s)
                        if 0 <= s - 1 < N:
                            exp_log(s - 1)
                        if 0 <= s - 3 < N:
                            weights(s - 3)

                @block.vector
                def _(dve):
                    for c in range(3):
                        dve.wait_ge(proj_full, 4 + c)
                        dve.tensor_copy(kT[:, c * CHUNK:(c + 1) * CHUNK], banks[3 + c][:, 0:CHUNK]).then_inc(k_kept, 1)
                    for g in range(3):
                        dve.wait_ge(kn_full, g + 1)
                        dve.tensor_copy(kn[:, 3 * g:3 * g + 3, :].rearrange("p t n -> p (t n)"), banks[1 + g][:, 0:CHUNK]).then_inc(kn_kept, 1)

                    def capped(n):
                        c0, c1 = first_col(steps[n]), width(steps[n])
                        dve.wait_ge(z_kept, n + 1)
                        if n >= NZ:
                            dve.wait_ge(sp_ready, n - NZ + 1)
                        dve.tensor_scalar(t[:, n % NZ, c0:c1], zs[:, n % NZ, c0:c1], 20.0, None, ALU.min).then_inc(t_capped, 1)

                    def softplus(n):
                        c0, c1 = first_col(steps[n]), width(steps[n])
                        dve.wait_ge(t_log, n + 1)
                        if n >= NZ:
                            dve.wait_ge(rest_added, n - NZ + 1)
                        dve.tensor_tensor(sp_[:, n % NZ, c0:c1], zs[:, n % NZ, c0:c1], t[:, n % NZ, c0:c1], ALU.max).then_inc(sp_ready, 1)

                    def exponent(n):
                        c0, c1 = first_col(steps[n]), width(steps[n])
                        dve.wait_ge(rest_full, n + 1)
                        dve.wait_ge(sp_ready, n + 1)
                        dve.tensor_tensor(zs[:, n % NZ, c0:c1], zs[:, n % NZ, c0:c1], rest[steps[n][0]][:, c0:c1], ALU.subtract).then_inc(e_ready, 1)

                    for s in range(N + 2):
                        if s < N:
                            capped(s)
                        if 0 <= s - 1 < N:
                            softplus(s - 1)
                        if 0 <= s - 2 < N:
                            exponent(s - 2)
                    dve.wait_ge(o_added, early_whole)
                    dve.wait_ge(o_added, late_whole)
                    dve.wait_ge(o_added, new_whole)
                    dve.tensor_copy(oB[:, HALF:PROMPT], o_late[:, :]).then_inc(o_kept, 1)
                    dve.tensor_copy(oB[:, 0:HALF], o_early[:, :]).then_inc(o_kept, 1)
                    for hh in range(2):
                        rows = slice(hh * HD, (hh + 1) * HD)
                        dve.tensor_copy(oB[rows, PROMPT:TOK].rearrange("p (s t) -> p s t", t=NEW),
                                        o_new[rows, 0:SC].rearrange("p (s h t) -> p s h t", s=SEQS, h=2)[:, :, hh, :]).then_inc(o_kept, 1)
            S.rest()


def gla_phase(nc, A, hT, oA_dram, prompt_state, sample_state):
    with ExitStack() as ctx:
        S = Scope(nc, ctx, "gla")
        ident = S.sb("ident", [P, P])
        causal = S.sb("causal", [P, 2, P])
        goes_on = S.sb("goes_on", [P, 2, TOK])
        own_rows = S.sb("own_rows", [P, SEQS])
        norm_w = S.sb("norm_w", [P, DV])
        w_lr, lrT = S.sb("w_lr", [P, KC, RANK]), S.sb("lrT", [RANK, TOK])
        w = S.sb("w", [P, KC, 2 * DK + 2 * DV])
        w_gate, b_gate = S.sb("w_gate", [RANK, DK]), S.sb("b_gate", [P, 1])
        qT, kT, la, b, c = (S.sb(n, [P, TOK]) for n in ("qT", "kT", "la", "b", "c"))
        eb, ec, kd = (S.sb(n, [P, TOK]) for n in ("eb", "ec", "kd"))
        v, og, o_raw = S.sb("v", [P, TILES, DV]), S.sb("og", [P, TILES, DV]), S.sb("o_raw", [P, TILES, DV])
        kl = S.sb("kl", [P, 2, SUBS, P])
        att = S.sb("att", [P, 2, P])
        kdn = S.sb("kdn", [P, 2, P])
        state = S.sb("state", [P, 2, DV])
        s0 = S.sb("s0", [P, SEQS, DV])
        v_own = S.sb("v_own", [P, SEQS, DV])
        q_own = S.sb("q_own", [P, SEQS * (P + NEW)])
        decay = S.sb("decay", [P, PTILES + SEQS])
        squares, rms, junk = S.sb("squares", [P, TILES]), S.sb("rms", [P, TILES]), S.sb("junk", [P, DV])
        oT = S.sb("oT", [P, 2, TOK])
        banks = [S.ps(f"bank{i}", [P, HALF]) for i in range(8)]

        const_in, w_in, lr_full, zeroed, gate_in, s0_in, proj_full, act_kept = (S.sem(n) for n in ("const_in", "w_in", "lr_full", "zeroed", "gate_in", "s0_in", "proj_full", "act_kept"))
        dve_kept, capped, gate_exp, gate_log, la_min, la_ready, b_ready, c_ready = (S.sem(n) for n in ("dve_kept", "capped", "gate_exp", "gate_log", "la_min", "la_ready", "b_ready", "c_ready"))
        eb_ready, ec_ready, decays, kd_diff, kd_exp, products, og_scaled, kl_exp = (S.sem(n) for n in ("eb_ready", "ec_ready", "decays", "kd_diff", "kd_exp", "products", "og_scaled", "kl_exp"))
        kl_ready, att_full, att_ready, kdT_full, kdn_ready, o_full, u_full, state_ready = (S.sem(n) for n in ("kl_ready", "att_full", "att_ready", "kdT_full", "kdn_ready", "o_full", "u_full", "state_ready"))
        o_kept, squared, v_split, q_split, s0_ready, mean_sq, mean_inv, root = (S.sem(n) for n in ("o_kept", "squared", "v_split", "q_split", "s0_ready", "mean_sq", "mean_inv", "root"))
        o_normed, oT_full, oT_kept, stored = (S.sem(n) for n in ("o_normed", "oT_full", "oT_kept", "stored"))
        kept = {"act_kept": act_kept, "dve_kept": dve_kept}

        N_CONST = 6
        with nc.Block() as block:

            @block.sync
            def _(sp):
                sp.dma_start(w_lr[:, :, :], A["w_lr"]).then_inc(gate_in, 16)
                for dst, src in ((ident, "ident"), (causal, "causal"), (own_rows, "own_rows")):
                    sp.dma_start(dst[:], A[src]).then_inc(const_in, 16)
                sp.dma_start(w[:, :, :], A["w_gla"][0]).then_inc(w_in, 16)
                sp.wait_ge(w_in, 16)
                sp.wait_ge(const_in, 16 * N_CONST)

            @block.scalar
            def _(act):
                for n in range(2):
                    act.dma_start(goes_on[:, n, :], A["goes_on"][n].partition_broadcast(P)).then_inc(const_in, 16)
                act.dma_start(norm_w[:, :], A["gla_norm"][0].partition_broadcast(P)).then_inc(const_in, 16)
                for g in range(CHUNKS):
                    act.wait_ge(lr_full, g + 1)
                    act.activation(lrT[:, g * CHUNK:(g + 1) * CHUNK], banks[g][0:RANK, 0:CHUNK], ACT.Copy).then_inc(act_kept, 1)

            @block.tensor
            def _(pe):
                pe.wait_ge(gate_in, 16)
                for g in range(CHUNKS):
                    for k in range(KC):
                        last = pe.matmul(banks[g][0:RANK, 0:CHUNK], w_lr[:, k, :], hT[:, k, g * CHUNK:(g + 1) * CHUNK], start=(k == 0), stop=(k == KC - 1))
                    last.then_inc(lr_full, 1)

            @block.vector
            def _(dve):
                dve.memset(kl[:, :, :, :], 0.0).then_inc(zeroed, 1)
                dve.memset(q_own[:, :], 0.0).then_inc(zeroed, 1)
        S.rest()

        groups = [("og", n) for n in range(5)] + [("gate", n) for n in range(3)] + [("q", n) for n in range(3)]
        groups += [("k", n) for n in range(3)] + [("v", n) for n in range(5)]
        keeper = {"og": "act_kept", "gate": "act_kept", "q": "act_kept", "k": "dve_kept", "v": "dve_kept"}
        count, kept_at = {"act_kept": 0, "dve_kept": 0}, []
        for what, _ in groups:
            count[keeper[what]] += 1
            kept_at.append((keeper[what], count[keeper[what]]))

        def two_tiles(n):
            return 1 if 2 * n + 1 == TILES else 2

        att_bank, kdT_bank, u_bank, o_bank, oT_bank = banks[0:2], banks[2], banks[3], banks[4:6], banks[6:8]
        by_tile = lambda x: x[:, 0:PROMPT].rearrange("p (t n) -> p t n", n=P)
        by_seq = lambda x: x[:, PROMPT:TOK].rearrange("p (s n) -> p s n", n=NEW)

        with nc.Fori(0, GLA_HEADS) as head:
            with nc.Block() as block:

                @block.sync
                def _(sp):
                    sp.dma_start(w_gate[:, :], A["w_gate"][:, bass.ds(head * DK, DK)]).then_inc(gate_in, 16)
                    sp.dma_start(b_gate[:, :], A["b_gate"][head]).then_inc(gate_in, 16)
                    sp.dma_start(s0[:, :, :], A["s0"][head]).then_inc(s0_in, 16)
                    sp.wait_ge(proj_full, len(groups))
                    sp.dma_start(w[:, :, :], A["w_gla"][head + 1]).then_inc(w_in, 16)
                    sp.wait_ge(state_ready, PTILES)
                    sp.dma_start(prompt_state[head], state[:, PTILES % 2, :]).then_inc(stored, 16)
                    sp.wait_ge(s0_ready, SEQS)
                    sp.dma_start(sample_state[head], s0[:, :, :]).then_inc(stored, 16)
                    sp.wait_ge(oT_kept, TILES)
                    sp.dma_start(oA_dram[bass.ds(2 * head, 2)].rearrange("k p t -> p k t"), oT[:, :, :]).then_inc(stored, 16)
                    sp.wait_ge(w_in, 16)
                    sp.wait_ge(stored, 48)

                @block.tensor
                def _(pe):
                    pe.wait_ge(gate_in, 32)
                    for g, (what, n) in enumerate(groups):
                        if g >= 8:
                            pe.wait_ge(kept[kept_at[g - 8][0]], kept_at[g - 8][1])
                        bank = banks[g % 8]
                        cols = slice(n * CHUNK, (n + 1) * CHUNK)
                        if what == "gate":
                            last = pe.matmul(bank[:, 0:CHUNK], w_gate[:, :], lrT[:, cols], start=True, stop=True)
                        elif what in "qk":
                            w0 = DK * "qk".index(what)
                            for k in range(KC):
                                last = pe.matmul(bank[:, 0:CHUNK], w[:, k, w0:w0 + DK], hT[:, k, cols], start=(k == 0), stop=(k == KC - 1))
                        else:
                            w0 = 2 * DK + DV * ["v", "og"].index(what)
                            for u in range(two_tiles(n)):
                                tile = 2 * n + u
                                for k in range(KC):
                                    last = pe.matmul(bank[:, u * DV:(u + 1) * DV], hT[:, k, tile * P:(tile + 1) * P], w[:, k, w0:w0 + DV],
                                                     start=(k == 0), stop=(k == KC - 1))
                        last.then_inc(proj_full, 1)
                    pe.wait_ge(act_kept, count["act_kept"])
                    pe.wait_ge(dve_kept, count["dve_kept"])
                    pe.wait_ge(products, 3)

                    def scores(n):
                        pe.wait_ge(kl_ready, n + 1)
                        if n >= 2:
                            pe.wait_ge(att_ready, n - 1)
                        for s in range(SUBS):
                            cols = slice(s * SUB, (s + 1) * SUB)
                            last = pe.matmul(att_bank[n % 2][:, cols], kl[:, n % 2, s, :], ec[:, n * P + s * SUB:n * P + (s + 1) * SUB], start=True, stop=True)
                        last.then_inc(att_full, 1)
                        if n >= 1:
                            pe.wait_ge(kdn_ready, n)
                        pe.transpose(kdT_bank[:, 0:P], kd[:, n * P:(n + 1) * P], ident[:, :]).then_inc(kdT_full, 1)

                    def outputs(n):
                        pe.wait_ge(att_ready, n + 1)
                        if n >= 2:
                            pe.wait_ge(o_kept, n - 1)
                        out = o_bank[n % 2][:, 0:DV]
                        last = pe.matmul(out, att[:, n % 2, :], v[:, n, :], start=True, stop=(n == 0))
                        if n:
                            pe.wait_ge(state_ready, n)
                            last = pe.matmul(out, eb[:, n * P:(n + 1) * P], state[:, n % 2, :], start=False, stop=True)
                        last.then_inc(o_full, 1)
                        pe.wait_ge(kdn_ready, n + 1)
                        pe.matmul(u_bank[:, 0:DV], kdn[:, n % 2, :], v[:, n, :], start=True, stop=True).then_inc(u_full, 1)

                    for s in range(PTILES + 2):
                        if s < PTILES:
                            scores(s)
                        if 0 <= s - 2:
                            outputs(s - 2)

                    n = PTILES
                    pe.wait_ge(kl_ready, n + 1)
                    pe.matmul(att_bank[n % 2][:, 0:P], kl[:, n % 2, 0, :], ec[:, PROMPT:TOK], start=True, stop=True).then_inc(att_full, 1)
                    pe.transpose(kdT_bank[:, 0:P], kd[:, PROMPT:TOK], ident[:, :]).then_inc(kdT_full, 1)
                    pe.wait_ge(att_ready, n + 1)
                    pe.wait_ge(o_kept, n - 1)
                    pe.wait_ge(s0_in, 16)
                    pe.wait_ge(q_split, 1)
                    out = o_bank[n % 2][:, 0:DV]
                    pe.matmul(out, att[:, n % 2, :], v[:, n, :], start=True, stop=False)
                    for s in range(SEQS):
                        last = pe.matmul(out, q_own[:, s * P:(s + 1) * P], s0[:, s, :], start=False, stop=(s == SEQS - 1))
                    last.then_inc(o_full, 1)
                    pe.wait_ge(kdn_ready, n + 1)
                    pe.wait_ge(v_split, SEQS)
                    for s in range(SEQS):
                        if s >= 2:
                            pe.wait_ge(s0_ready, s - 1)
                        else:
                            pe.wait_ge(state_ready, PTILES)
                        pe.matmul((u_bank, kdT_bank)[s % 2][:, 0:DV], kdn[:, n % 2, :], v_own[:, s, :], start=True, stop=True).then_inc(u_full, 1)

                    for t in range(TILES):
                        pe.wait_ge(o_normed, t + 1)
                        if t >= 2:
                            pe.wait_ge(oT_kept, t - 1)
                        for k in range(2):
                            last = pe.transpose(oT_bank[t % 2][:, k * P:(k + 1) * P], o_raw[:, t, k * P:(k + 1) * P], ident[:, :])
                        last.then_inc(oT_full, 1)

                @block.scalar
                def _(act):
                    for g, (what, n) in enumerate(groups):
                        if keeper[what] != "act_kept":
                            continue
                        act.wait_ge(proj_full, g + 1)
                        cols, bank = slice(n * CHUNK, (n + 1) * CHUNK), banks[g % 8]
                        if what == "og":
                            m = two_tiles(n)
                            act.activation(og[:, 2 * n:2 * n + m, :].rearrange("p t n -> p (t n)"), bank[:, 0:m * DV], ACT.Silu).then_inc(act_kept, 1)
                        elif what == "gate":
                            act.activation(la[:, cols], bank[:, 0:CHUNK], ACT.Identity, bias=b_gate[:, 0:1]).then_inc(act_kept, 1)
                        else:
                            act.activation(qT[:, cols], bank[:, 0:CHUNK], ACT.Copy, scale=DK ** -0.5).then_inc(act_kept, 1)
                    act.preload_act_table_set("natural_log_exp_and_others")
                    act.wait_ge(capped, 1)
                    act.activation(b[:, :], b[:, :], ACT.Exp, scale=-1.0).then_inc(gate_exp, 1)
                    act.wait_ge(gate_exp, 1)
                    act.activation(b[:, :], b[:, :], ACT.Ln, bias=1.0).then_inc(gate_log, 1)
                    act.wait_ge(b_ready, 1)
                    act.wait_ge(c_ready, 1)
                    act.activation(ec[:, :], c[:, :], ACT.Exp).then_inc(ec_ready, 1)
                    act.activation(eb[:, :], b[:, :], ACT.Exp).then_inc(eb_ready, 1)
                    act.activation(decay[:, 0:PTILES], by_tile(b)[:, :, P - 1], ACT.Exp).then_inc(decays, 1)
                    act.activation(decay[:, PTILES:], by_seq(b)[:, :, NEW - 1], ACT.Exp).then_inc(decays, 1)
                    act.wait_ge(kd_diff, 2)
                    act.activation(kd[:, :], kd[:, :], ACT.Exp).then_inc(kd_exp, 1)

                    def key_scales(n):
                        if n >= 2:
                            act.wait_ge(att_full, n - 1)
                        for s in range(SUBS):
                            here = n * P
                            before = b[:, here + s * SUB - 1:here + s * SUB] if s else 0.0
                            last = act.activation(kl[:, n % 2, s, 0:(s + 1) * SUB], b[:, here:here + (s + 1) * SUB], ACT.Exp, bias=before, scale=-1.0)
                        last.then_inc(kl_exp, 1)

                    def rest(n):
                        act.wait_ge(kdT_full, n + 1)
                        if n >= 2:
                            act.wait_ge(u_full, n - 1)
                        act.activation(kdn[:, n % 2, :], kdT_bank[:, 0:P], ACT.Copy).then_inc(kdn_ready, 1)

                    def square(n):
                        act.wait_ge(o_kept, n + 1)
                        if n:
                            act.wait_ge(squared, n)
                        act.activation(junk[:, :], o_raw[:, n, :], ACT.Square, accum_out=squares[:, n:n + 1]).then_inc(squared, 1)

                    for s in range(PTILES + 3):
                        if s < PTILES:
                            key_scales(s)
                        if 0 <= s - 1 < PTILES:
                            rest(s - 1)
                        if 0 <= s - 3:
                            square(s - 3)
                    n = PTILES
                    act.wait_ge(att_full, n - 1)
                    act.activation(kl[:, n % 2, 0, :], c[:, PROMPT:TOK], ACT.Exp, scale=-1.0).then_inc(kl_exp, 1)
                    rest(n)
                    square(n)
                    act.wait_ge(mean_inv, 1)
                    act.activation(rms[:, :], rms[:, :], ACT.Sqrt).then_inc(root, 1)
                    for t in range(TILES):
                        act.wait_ge(oT_full, t + 1)
                        act.activation(oT[:, :, t * P:(t + 1) * P], oT_bank[t % 2][:, 0:2 * P].rearrange("p (k n) -> p k n", k=2), ACT.Copy).then_inc(oT_kept, 1)

                @block.vector
                def _(dve):
                    for g, (what, n) in enumerate(groups):
                        if keeper[what] == "dve_kept":
                            dve.wait_ge(proj_full, g + 1)
                            bank = banks[g % 8]
                            if what == "k":
                                dve.tensor_copy(kT[:, n * CHUNK:(n + 1) * CHUNK], bank[:, 0:CHUNK]).then_inc(dve_kept, 1)
                            else:
                                m = two_tiles(n)
                                dve.tensor_copy(v[:, 2 * n:2 * n + m, :].rearrange("p t n -> p (t n)"), bank[:, 0:m * DV]).then_inc(dve_kept, 1)
                        if g == 9:
                            dve.wait_ge(act_kept, 8)
                            dve.tensor_scalar(b[:, :], la[:, :], -20.0, None, ALU.max).then_inc(capped, 1)
                        if g == 13:
                            dve.wait_ge(gate_log, 1)
                            dve.scalar_tensor_tensor(la[:, :], b[:, :], -1.0, la[:, :], ALU.mult, ALU.min).then_inc(la_min, 1)
                            dve.wait_ge(la_min, 1)
                            dve.tensor_scalar(la[:, :], la[:, :], 1.0 / TAU, None, ALU.mult).then_inc(la_ready, 1)
                            dve.wait_ge(la_ready, 1)
                            dve.tensor_tensor_scan(b[:, :], goes_on[:, 0, :], la[:, :], 0.0, ALU.mult, ALU.add).then_inc(b_ready, 1)
                            dve.tensor_tensor_scan(c[:, :], goes_on[:, 1, :], la[:, :], 0.0, ALU.mult, ALU.add).then_inc(c_ready, 1)
                    for s in range(SEQS):
                        if s == 0:
                            dve.wait_ge(dve_kept, count["dve_kept"])
                        dve.tensor_scalar(v_own[:, s, :], v[:, TILES - 1, :], own_rows[:, s:s + 1], None, ALU.mult).then_inc(v_split, 1)
                    dve.wait_ge(b_ready, 1)
                    for x, out in ((by_tile(b), by_tile(kd)), (by_seq(b), by_seq(kd))):
                        last = x[:, :, x.shape[2] - 1:x.shape[2]].broadcast_to(x.shape)
                        dve.tensor_tensor(out, last, x, ALU.subtract).then_inc(kd_diff, 1)
                    dve.wait_ge(act_kept, count["act_kept"])
                    dve.wait_ge(ec_ready, 1)
                    dve.tensor_tensor(ec[:, :], ec[:, :], qT[:, :], ALU.mult).then_inc(products, 1)
                    dve.wait_ge(eb_ready, 1)
                    dve.tensor_tensor(eb[:, :], eb[:, :], qT[:, :], ALU.mult).then_inc(products, 1)
                    dve.wait_ge(kd_exp, 1)
                    dve.tensor_tensor(kd[:, :], kd[:, :], kT[:, :], ALU.mult).then_inc(products, 1)
                    dve.wait_ge(products, 2)
                    dve.tensor_copy(q_own[:, :].rearrange("p (s n) -> p s n", n=P + NEW)[:, :, 0:NEW], by_seq(eb)).then_inc(q_split, 1)
                    dve.tensor_tensor(og[:, :, :], og[:, :, :], norm_w[:, :].unsqueeze(1).broadcast_to([P, TILES, DV]), ALU.mult).then_inc(og_scaled, 1)

                    def scale_keys(n):
                        dve.wait_ge(kl_exp, n + 1)
                        if n < PTILES:
                            keys = kT[:, n * P:(n + 1) * P].unsqueeze(1).broadcast_to([P, SUBS, P])
                            dve.tensor_tensor(kl[:, n % 2], kl[:, n % 2], keys, ALU.mult).then_inc(kl_ready, 1)
                        else:
                            dve.tensor_tensor(kl[:, n % 2, 0, :], kl[:, n % 2, 0, :], kT[:, PROMPT:TOK], ALU.mult).then_inc(kl_ready, 1)

                    def hide_future(n):
                        dve.wait_ge(att_full, n + 1)
                        if n >= 2:
                            dve.wait_ge(o_full, n - 1)
                        dve.tensor_tensor(att[:, n % 2, :], att_bank[n % 2][:, 0:P], causal[:, n // PTILES, :], ALU.mult).then_inc(att_ready, 1)

                    def next_state(n):
                        dve.wait_ge(u_full, n + 1)
                        if n == 0:
                            dve.tensor_copy(state[:, 1, :], u_bank[:, 0:DV]).then_inc(state_ready, 1)
                        else:
                            dve.wait_ge(state_ready, n)
                            dve.wait_ge(decays, 1)
                            dve.scalar_tensor_tensor(state[:, (n + 1) % 2, :], state[:, n % 2, :], decay[:, n:n + 1], u_bank[:, 0:DV],
                                                     ALU.mult, ALU.add).then_inc(state_ready, 1)

                    def keep_output(n):
                        dve.wait_ge(o_full, n + 1)
                        dve.tensor_copy(o_raw[:, n, :], o_bank[n % 2][:, 0:DV]).then_inc(o_kept, 1)

                    for s in range(PTILES + 3):
                        if 0 <= s - 3:
                            next_state(s - 3)
                            keep_output(s - 3)
                        if s < PTILES:
                            scale_keys(s)
                        if 0 <= s - 1 < PTILES:
                            hide_future(s - 1)
                    n = PTILES
                    scale_keys(n)
                    hide_future(n)
                    keep_output(n)
                    for s in range(SEQS):
                        dve.wait_ge(u_full, PTILES + s + 1)
                        dve.wait_ge(decays, 2)
                        dve.scalar_tensor_tensor(s0[:, s, :], s0[:, s, :], decay[:, PTILES + s:PTILES + s + 1], (u_bank, kdT_bank)[s % 2][:, 0:DV],
                                                 ALU.mult, ALU.add).then_inc(s0_ready, 1)
                    dve.wait_ge(squared, TILES)
                    dve.tensor_scalar(rms[:, :], squares[:, :], 1.0 / DV, RMS_EPS, ALU.mult, ALU.add).then_inc(mean_sq, 1)
                    dve.wait_ge(mean_sq, 1)
                    dve.reciprocal(rms[:, :], rms[:, :]).then_inc(mean_inv, 1)
                    dve.wait_ge(root, 1)
                    dve.wait_ge(og_scaled, 1)
                    dve.wait_ge(o_kept, TILES)
                    for t in range(TILES):
                        dve.scalar_tensor_tensor(o_raw[:, t, :], o_raw[:, t, :], rms[:, t:t + 1], og[:, t, :], ALU.mult, ALU.mult).then_inc(o_normed, 1)
            S.rest()


def mix_phase(nc, A, hT, oA_dram, oB_dram, mixT_dram):
    with ExitStack() as ctx:
        S = Scope(nc, ctx, "mix")
        oA, oB = S.sb("oA", [P, KC, TOK]), S.sb("oB", [P, KC, TOK])
        w = S.sb("w", [P, 4, KC, P])
        sg = S.sb("sg", [P, 2, 2, CHUNK])
        part = S.sb("part", [P, 2, 2, CHUNK])
        mixed = S.sb("mixed", [P, TOK])
        banks = [S.ps(f"bank{i}", [P, HALF]) for i in range(8)]
        o_in, w_in = S.sem("o_in"), S.sem("w_in")
        full, gated, parts, mixed_ready, stored = S.sem("full"), S.sem("gated"), S.sem("parts"), S.sem("mixed_ready"), S.sem("stored")
        with nc.Block() as block:

            @block.sync
            def _(sp):
                sp.dma_start(w[:, :, :, :], A["w_mix"][0]).then_inc(w_in, 16)
                sp.dma_start(oA[:, :, :], oA_dram.rearrange("k p t -> p k t")).then_inc(o_in, 16)
                sp.dma_start(oB[:, :, :], oB_dram.rearrange("k p t -> p k t")).then_inc(o_in, 16)
                sp.wait_ge(w_in, 16)
                sp.wait_ge(o_in, 32)
        S.rest()
        with nc.Fori(0, KC) as j:
            with nc.Block() as block:

                @block.sync
                def _(sp):
                    sp.wait_ge(full, 4 * CHUNKS)
                    sp.dma_start(w[:, :, :, :], A["w_mix"][j + 1]).then_inc(w_in, 16)
                    sp.wait_ge(mixed_ready, CHUNKS)
                    sp.dma_start(mixT_dram[j], mixed[:, :]).then_inc(stored, 16)
                    sp.wait_ge(w_in, 16)
                    sp.wait_ge(stored, 16)

                @block.tensor
                def _(pe):
                    for c in range(CHUNKS):
                        if c >= 2:
                            pe.wait_ge(gated, 2 * (c - 1))
                            pe.wait_ge(parts, 2 * (c - 1))
                        for m, x in enumerate((hT, hT, oA, oB)):
                            for k in range(KC):
                                last = pe.matmul(banks[4 * (c % 2) + m][:, 0:CHUNK], w[:, m, k, :], x[:, k, c * CHUNK:(c + 1) * CHUNK],
                                                 start=(k == 0), stop=(k == KC - 1))
                            last.then_inc(full, 1)

                @block.scalar
                def _(act):
                    for c in range(CHUNKS):
                        for m in range(2):
                            act.wait_ge(full, 4 * c + m + 1)
                            if c >= 2:
                                act.wait_ge(parts, 2 * (c - 2) + m + 1)
                            act.activation(sg[:, c % 2, m, :], banks[4 * (c % 2) + m][:, 0:CHUNK], ACT.Sigmoid).then_inc(gated, 1)

                @block.vector
                def _(dve):
                    for c in range(CHUNKS):
                        for m in range(2):
                            dve.wait_ge(full, 4 * c + m + 3)
                            dve.wait_ge(gated, 2 * c + m + 1)
                            if c >= 2:
                                dve.wait_ge(mixed_ready, c - 1)
                            dve.tensor_tensor(part[:, c % 2, m, :], sg[:, c % 2, m, :], banks[4 * (c % 2) + 2 + m][:, 0:CHUNK], ALU.mult).then_inc(parts, 1)
                        dve.wait_ge(parts, 2 * c + 2)
                        dve.tensor_tensor(mixed[:, c * CHUNK:(c + 1) * CHUNK], part[:, c % 2, 0, :], part[:, c % 2, 1, :], ALU.add).then_inc(mixed_ready, 1)
            S.rest()


def residual_phase(nc, A, modb, mixT_dram, x1_dram, h2_dram, h2T_dram):
    U = 3
    MW = 3 * D
    with ExitStack() as ctx:
        S = Scope(nc, ctx, "res")
        ident, w_o = S.sb("ident", [P, P]), S.sb("w_o", [P, KC, D])
        ln1 = S.sb("ln1", [P, 2 * D])
        mods = S.sb("mods", [P, 2, MW])
        mT = S.sb("mT", [P, U, KC, P])
        x, x1, h2 = S.sb("x", [P, U, D]), S.sb("x1", [P, U, D]), S.sb("h2", [P, U, D])
        h2T = S.sb("h2T", [P, U, KC, P])
        stats, mv, rstd = S.sb("stats", [P, 2 * U, 2, 6]), S.sb("mv", [P, 2 * U, 2]), S.sb("rstd", [P, 2 * U])
        y = [[S.ps(f"y{i}{c}", [P, HALF]) for c in range(2)] for i in range(2)]
        turned = [S.ps(f"turned{i}", [P, 4, P]) for i in range(2)]
        const_in, mods_in = S.sem("const_in"), S.sem("mods_in")
        m_in, x_in = [S.sem(f"m_in{u}") for u in range(U)], [S.sem(f"x_in{u}") for u in range(U)]
        y_full, y_used, summed, normed, inverse, x1_steps, h2_steps = (S.sem(n) for n in ("y_full", "y_used", "summed", "normed", "inverse", "x1_steps", "h2_steps"))
        turned_full, h2T_kept, stored = S.sem("turned_full"), S.sem("h2T_kept"), S.sem("stored")
        tiles = lambda a: a.rearrange("(t p) n -> t p n", p=P)
        with nc.Block() as block:

            @block.sync
            def _(sp):
                sp.dma_start(w_o[:, :, :], A["w_o"]).then_inc(const_in, 16)
                sp.dma_start(ident[:, :], A["ident"]).then_inc(const_in, 16)
                sp.dma_start(mods[:, 0, :], modb[0, :, 2 * D:5 * D]).then_inc(const_in, 16)
                sp.dma_start(ln1[:, :], A["ln1"][0].partition_broadcast(P)).then_inc(const_in, 16)
                sp.wait_ge(const_in, 64)
        S.rest()
        with nc.Fori(0, TILES // U) as i:
            with nc.Block() as block:

                @block.sync
                def _(sp):
                    for u in range(U):
                        sp.dma_start(mT[:, u], mixT_dram.rearrange("k p t -> p k t")[:, :, bass.ds(U * P * i + P * u, P)]).then_inc(m_in[u], 16)
                        sp.dma_start(x[:, u, :], tiles(A["x"])[U * i + u]).then_inc(x_in[u], 16)
                    sp.dma_start(mods[:, 1, :], modb[i // 2, :, 2 * D:5 * D]).then_inc(mods_in, 16)
                    for u in range(U):
                        sp.wait_ge(x1_steps, 2 * u + 2)
                        sp.dma_start(tiles(x1_dram)[U * i + u], x1[:, u, :]).then_inc(stored, 16)
                        sp.wait_ge(h2_steps, 2 * u + 2)
                        sp.dma_start(tiles(h2_dram)[U * i + u], h2[:, u, :]).then_inc(stored, 16)
                        sp.wait_ge(h2T_kept, 2 * u + 2)
                        sp.dma_start(h2T_dram[U * i + u], h2T[:, u].rearrange("p k n -> p (k n)")).then_inc(stored, 16)
                    sp.wait_ge(stored, 16 * 3 * U)

                @block.tensor
                def _(pe):
                    def turn(u):
                        pe.wait_ge(h2_steps, 2 * u + 2)
                        for c in range(2):
                            n = 2 * u + c
                            if n >= 2:
                                pe.wait_ge(h2T_kept, n - 1)
                            for k in range(4):
                                last = pe.transpose(turned[c][:, k, :], h2[:, u, (4 * c + k) * P:(4 * c + k + 1) * P], ident[:, :])
                            last.then_inc(turned_full, 1)

                    for u in range(U):
                        pe.wait_ge(m_in[u], 16)
                        if u >= 2:
                            pe.wait_ge(y_used, 2 * (u - 1))
                        for c in range(2):
                            for k in range(KC):
                                last = pe.matmul(y[u % 2][c][:, :], mT[:, u, k, :], w_o[:, k, c * HALF:(c + 1) * HALF], start=(k == 0), stop=(k == KC - 1))
                            last.then_inc(y_full, 1)
                        if u:
                            turn(u - 1)
                    turn(U - 1)

                @block.scalar
                def _(act):
                    def root(n):
                        act.wait_ge(normed, 6 * n + 5)
                        act.activation(rstd[:, n:n + 1], rstd[:, n:n + 1], ACT.Sqrt).then_inc(inverse, 1)

                    for u in range(U):
                        root(2 * u)
                        root(2 * u + 1)
                        for c in range(2):
                            act.wait_ge(turned_full, 2 * u + c + 1)
                            act.activation(h2T[:, u, 4 * c:4 * c + 4, :], turned[c][:, :, :], ACT.Copy).then_inc(h2T_kept, 1)

                @block.vector
                def _(dve):
                    n = 0
                    for u in range(U):
                        m = mods[:, u // 2, :]
                        if u == 2:
                            dve.wait_ge(mods_in, 16)
                        for c in range(2):
                            dve.wait_ge(y_full, 2 * u + c + 1)
                            dve.tensor_tensor(x1[:, u, c * HALF:(c + 1) * HALF], y[u % 2][c][:, :], m[:, c * HALF:(c + 1) * HALF], ALU.mult).then_inc(y_used, 1)
                        dve.wait_ge(x_in[u], 16)
                        dve.wait_ge(y_used, 2 * u + 2)
                        dve.scalar_tensor_tensor(x[:, u, :], x[:, u, :], ALPHA, x1[:, u, :], ALU.mult, ALU.add).then_inc(summed, 1)
                        dve.wait_ge(summed, u + 1)
                        n = layer_norm_steps(dve, normed, inverse, 2 * u, n, x[:, u, :], stats[:, 2 * u], mv[:, 2 * u], rstd[:, 2 * u:2 * u + 1], x[:, u, :])
                        dve.wait_ge(normed, n)
                        dve.tensor_tensor(x1[:, u, :], x[:, u, :], ln1[:, 0:D], ALU.mult).then_inc(x1_steps, 1)
                        dve.wait_ge(x1_steps, 2 * u + 1)
                        dve.tensor_tensor(x1[:, u, :], x1[:, u, :], ln1[:, D:2 * D], ALU.add).then_inc(x1_steps, 1)
                        dve.wait_ge(x1_steps, 2 * u + 2)
                        n = layer_norm_steps(dve, normed, inverse, 2 * u + 1, n, x1[:, u, :], stats[:, 2 * u + 1], mv[:, 2 * u + 1], rstd[:, 2 * u + 1:2 * u + 2], h2[:, u, :])
                        dve.wait_ge(normed, n)
                        dve.scalar_tensor_tensor(h2[:, u, :], m[:, 2 * D:3 * D], 1.0, h2[:, u, :], ALU.add, ALU.mult).then_inc(h2_steps, 1)
                        dve.wait_ge(h2_steps, 2 * u + 1)
                        dve.tensor_tensor(h2[:, u, :], h2[:, u, :], m[:, D:2 * D], ALU.add).then_inc(h2_steps, 1)
            S.rest()


def peer_phase(nc, A, modb, x1_dram, h2_dram, h2T_dram, y_out):
    SLOTS = PEER_HEADS * TOPK
    U = 3
    R = 8
    G = 1
    DG = 8
    with ExitStack() as ctx:
        S = Scope(nc, ctx, "peer")
        ident = S.sb("ident", [P, P])
        w_q, keysT = S.sb("w_q", [P, KC, 2 * PEER_HEADS * P]), S.sb("keysT", [P, 2 * PEER_HEADS, NKEYS])
        ln2 = S.sb("ln2", [P, 2 * D])
        sixteen = S.sb("sixteen", [P, TOPK])
        ring = S.sb("ring", [P, R, 2 * D])
        h2, x1, g2 = S.sb("h2", [P, U, D]), S.sb("x1", [P, 2, D]), S.sb("g2", [P, 2, D])
        h2T = S.sb("h2T", [P, U, KC, P])
        diag = S.sb("diag", [P, DG, P])
        dots, act_v, w = S.sb("dots", [P, SLOTS]), S.sb("act_v", [P, SLOTS]), S.sb("w", [P, SLOTS])
        experts, gates = S.sb("experts", [P, U, SLOTS], U32), S.sb("gates", [P, U, SLOTS])
        qs = S.sb("qs", [P, 2, 2, P])
        sc, sc2 = S.sb("sc", [P, 2, 2, NKEYS]), S.sb("sc2", [P, 2, NKEYS])
        top, at = S.sb("top", [P, 2, TOPK]), S.sb("at", [P, 2, TOPK], U32)
        at_f = S.sb("at_f", [P, 2, TOPK])
        cand, cand2 = S.sb("cand", [P, TOPK, TOPK]), S.sb("cand2", [P, TOPK * TOPK])
        best, pos = S.sb("best", [P, TOPK]), S.sb("pos", [P, TOPK], U32)
        part, part_f = S.sb("part", [P, 2, TOPK], U32), S.sb("part_f", [P, 2, TOPK])
        hit = S.sb("hit", [P, 2, TOPK, TOPK])
        ids = S.sb("ids", [P, 2, TOPK])
        shifted, e_sum, e_inv = S.sb("shifted", [P, TOPK]), S.sb("e_sum", [P, 1]), S.sb("e_inv", [P, 1])
        stats, mv, rstd = S.sb("stats", [P, 2, 6]), S.sb("mv", [P, 2]), S.sb("rstd", [P, 1])
        f = [[S.ps(f"f{b}{c}", [P, HALF]) for c in range(2)] for b in range(2)]
        q_bank = [S.ps(f"q{i}", [P, 2, P]) for i in range(2)]
        s_bank = [S.ps(f"s{i}", [P, 2, NKEYS]) for i in range(2)]

        const_in, gate2_in, next_in = S.sem("const_in"), S.sem("gate2_in"), S.sem("next_in")
        h2T_in, h2_in, x1_in = ([S.sem(f"{n}{u}") for u in range(U)] for n in ("h2T_in", "h2_in", "x1_in"))
        w_q_in = [S.sem(f"w_q_in{n}") for n in range(2)]
        ring_in = [S.sem(f"ring_in{r}") for r in range(R)]
        dot_done, gelu_done, w_ready, diag_ready, v_used = (S.sem(n) for n in ("dot_done", "gelu_done", "w_ready", "diag_ready", "v_used"))
        q_full, q_kept, s_full, s_kept = (S.sem(n) for n in ("q_full", "q_kept", "s_full", "s_kept"))
        chosen, exp_done = S.sem("chosen"), S.sem("exp_done")
        f_read, normed, inverse, ended, stored = S.sem("f_read"), S.sem("normed"), S.sem("inverse"), S.sem("ended"), S.sem("stored")

        GROUPS = SLOTS // G
        END = 4 // G - 1
        KEYS_AT, PARTS_AT, EXP_AT = 4, 8, 12

        def query_matmuls(pe, h, tile):
            head = h % PEER_HEADS
            if h >= 2:
                pe.wait_ge(q_kept, h - 1)
            for p in range(2):
                for k in range(KC):
                    last = pe.matmul(q_bank[h % 2][:, p, :], w_q[:, k, (2 * head + p) * P:(2 * head + p + 1) * P], h2T[:, tile, k, :], start=(k == 0), stop=(k == KC - 1))
            last.then_inc(q_full, 1)

        def key_matmuls(pe, h):
            pe.wait_ge(q_kept, h + 1)
            if h >= 2:
                pe.wait_ge(s_kept, h - 1)
            for p in range(2):
                last = pe.matmul(s_bank[h % 2][:, p, :], qs[:, h % 2, p, :], keysT[:, 2 * (h % PEER_HEADS) + p, :], start=True, stop=True)
            last.then_inc(s_full, 1)

        def keep_query(act, h):
            act.wait_ge(q_full, h + 1)
            if h >= 2:
                act.wait_ge(s_full, h - 1)
            act.activation(qs[:, h % 2], q_bank[h % 2][:, :, :], ACT.Copy).then_inc(q_kept, 1)

        def keep_scores(act, h):
            act.wait_ge(s_full, h + 1)
            if h >= 2:
                act.wait_ge(chosen, CHOOSE * (h - 1))
            act.activation(sc[:, h % 2], s_bank[h % 2][:, :, :], ACT.Copy).then_inc(s_kept, 1)

        def exp_best(act, h):
            act.wait_ge(chosen, CHOOSE * h + SHIFTED)
            act.activation(shifted[:, :], shifted[:, :], ACT.Exp, accum_out=e_sum[:, 0:1]).then_inc(exp_done, 1)

        CHOOSE, PARTS, SHIFTED = 27, 11, 18

        def counting(dve, step):
            def did(ins):
                ins.then_inc(chosen, 1)
                step[0] += 1

            def so_far(back=0):
                dve.wait_ge(chosen, step[0] - back)

            return did, so_far

        def choose_parts(dve, h):

            step = [CHOOSE * h]
            did, so_far = counting(dve, step)
            s = sc[:, h % 2]
            dve.wait_ge(s_kept, h + 1)
            so_far()
            for p in range(2):
                did(dve.max(top[:, p, 0:8], s[:, p, :]))
            for p in range(2):
                so_far(1)
                did(dve.max_index(at[:, p, 0:8], top[:, p, 0:8], s[:, p, :]))
                did(dve.match_replace(sc2[:, p, :], top[:, p, 0:8], s[:, p, :], NEG))
            so_far()
            for p in range(2):
                did(dve.max(top[:, p, 8:16], sc2[:, p, :]))
            so_far()
            for p in range(2):
                did(dve.max_index(at[:, p, 8:16], top[:, p, 8:16], sc2[:, p, :]))
            did(dve.tensor_tensor(cand[:, :, :], top[:, 0, :].unsqueeze(2).broadcast_to([P, TOPK, TOPK]),
                                  top[:, 1, :].unsqueeze(1).broadcast_to([P, TOPK, TOPK]), ALU.add))
            assert step[0] == CHOOSE * h + PARTS

        def choose_best(dve, h, tile):
            step = [CHOOSE * h + PARTS]
            did, so_far = counting(dve, step)
            so_far()
            flat = cand[:, :, :].rearrange("p i j -> p (i j)")
            did(dve.max(best[:, 0:8], flat))
            did(dve.tensor_copy(at_f[:, :, :], at[:, :, :]))
            so_far()
            did(dve.match_replace(cand2[:, :], best[:, 0:8], flat, NEG))
            did(dve.max_index(pos[:, 0:8], best[:, 0:8], flat))
            so_far()
            did(dve.max(best[:, 8:16], cand2[:, :]))
            so_far()
            did(dve.max_index(pos[:, 8:16], best[:, 8:16], cand2[:, :]))
            did(dve.tensor_scalar(shifted[:, :], best[:, :], best[:, 0:1], None, ALU.subtract))
            assert step[0] == CHOOSE * h + SHIFTED
            so_far(1)
            did(dve.tensor_single_scalar(part[:, 0, :], pos[:, :], 4, ALU.logical_shift_right))
            did(dve.tensor_single_scalar(part[:, 1, :], pos[:, :], TOPK - 1, ALU.bitwise_and))
            so_far()
            did(dve.tensor_copy(part_f[:, :, :], part[:, :, :]))
            so_far()
            did(dve.tensor_tensor(hit[:, :, :, :].rearrange("p a i j -> p (a i) j"), part_f[:, :, :].rearrange("p a i -> p (a i)").unsqueeze(2).broadcast_to([P, 2 * TOPK, TOPK]),
                                  sixteen[:, :].unsqueeze(1).broadcast_to([P, 2 * TOPK, TOPK]), ALU.is_equal))
            so_far()
            did(dve.tensor_tensor(hit[:, :, :, :], hit[:, :, :, :], at_f[:, :, :].unsqueeze(2).broadcast_to([P, 2, TOPK, TOPK]), ALU.mult))
            so_far()
            did(dve.tensor_reduce(ids[:, :, :].rearrange("p a i -> p (a i)"), hit[:, :, :, :].rearrange("p a i j -> p (a i) j"), AX_X, ALU.add))
            dve.wait_ge(exp_done, h + 1)
            did(dve.reciprocal(e_inv[:, :], e_sum[:, :]))
            so_far()
            cols = slice(h % PEER_HEADS * TOPK, (h % PEER_HEADS + 1) * TOPK)
            did(dve.scalar_tensor_tensor(experts[:, tile, cols], ids[:, 0, :], float(NKEYS), ids[:, 1, :], ALU.mult, ALU.add))
            did(dve.tensor_scalar(gates[:, tile, cols], shifted[:, :], e_inv[:, 0:1], None, ALU.mult))
            assert step[0] == CHOOSE * (h + 1)

        def fetch(pool, slot, tile, k):
            pool.indirect_dma_start(ring[:, slot % R, :], None, A["uv"], bass.IndirectOffsetOnAxis(ap=experts[:, tile, k:k + 1], axis=0)).then_inc(ring_in[slot % R], 16)

        def rest_fetches(pool, each):
            for r in range(R):
                pool.wait_ge(ring_in[r], 16 * each)
            pool.dma_reset(range(ring_in[0].num, ring_in[-1].num + 1))

        rows = lambda a: a.rearrange("(t p) n -> t p n", p=P)
        flat_h2T = lambda u: h2T[:, u].rearrange("p k n -> p (k n)")
        with nc.Block() as block:

            @block.sync
            def _(sp):
                sp.dma_start(flat_h2T(0), h2T_dram[0]).then_inc(h2T_in[0], 16)
                for n, cols in enumerate((slice(0, 2 * P), slice(2 * P, 2 * PEER_HEADS * P))):
                    sp.dma_start(w_q[:, :, cols], A["w_q"][:, :, cols]).then_inc(w_q_in[n], 16)
                    if n == 0:
                        sp.dma_start(keysT[:, :, :], A["keysT"]).then_inc(const_in, 16)
                        sp.dma_start(sixteen[:, :], A["sixteen"]).then_inc(const_in, 16)
                sp.dma_start(ident[:, :], A["ident"]).then_inc(next_in, 16)
                sp.dma_start(ln2[:, :], A["ln2"][0].partition_broadcast(P)).then_inc(next_in, 16)
                sp.dma_start(flat_h2T(1), h2T_dram[1]).then_inc(next_in, 16)
                sp.dma_start(h2[:, 0, :], rows(h2_dram)[0]).then_inc(next_in, 16)
                sp.dma_start(g2[:, 0, :], modb[0, :, 5 * D:6 * D]).then_inc(next_in, 16)
                sp.wait_ge(next_in, 80)

            @block.gpsimd
            def _(pool):
                pool.wait_ge(chosen, CHOOSE)
                for r in range(R):
                    fetch(pool, r, 0, r)
                rest_fetches(pool, 1)

            @block.tensor
            def _(pe):
                pe.wait_ge(h2T_in[0], 16)
                for h in range(PEER_HEADS):
                    if h < 2:
                        pe.wait_ge(w_q_in[h], 16)
                    query_matmuls(pe, h, 0)
                    if h == 1:
                        pe.wait_ge(const_in, 32)
                    if h:
                        key_matmuls(pe, h - 1)
                key_matmuls(pe, PEER_HEADS - 1)

            @block.scalar
            def _(act):
                for h in range(PEER_HEADS):
                    keep_query(act, h)
                    keep_scores(act, h)
                    exp_best(act, h)

            @block.vector
            def _(dve):
                dve.wait_ge(const_in, 32)
                for h in range(PEER_HEADS):
                    choose_parts(dve, h)
                    choose_best(dve, h, 0)
        S.rest()

        with nc.Fori(0, TILES // U) as i:
            with nc.Block() as block:

                @block.sync
                def _(sp):
                    sp.dma_start(flat_h2T(2), h2T_dram[U * i + 2]).then_inc(h2T_in[2], 16)
                    sp.dma_start(h2[:, 1, :], rows(h2_dram)[U * i + 1]).then_inc(h2_in[1], 16)
                    sp.dma_start(g2[:, 1, :], modb[i // 2, :, 5 * D:6 * D]).then_inc(gate2_in, 16)
                    sp.dma_start(x1[:, 0, :], rows(x1_dram)[U * i]).then_inc(x1_in[0], 16)
                    sp.dma_start(x1[:, 1, :], rows(x1_dram)[U * i + 1]).then_inc(x1_in[1], 16)
                    sp.dma_start(flat_h2T(0), h2T_dram[(U * i + U) % TILES]).then_inc(h2T_in[0], 16)
                    sp.dma_start(h2[:, 2, :], rows(h2_dram)[U * i + 2]).then_inc(h2_in[2], 16)
                    sp.wait_ge(q_full, PEER_HEADS)
                    sp.dma_start(flat_h2T(1), h2T_dram[(U * i + U + 1) % TILES]).then_inc(next_in, 16)
                    for u in range(U):
                        sp.wait_ge(ended, 3 * u + 3)
                        sp.dma_start(rows(y_out)[U * i + u], x1[:, u % 2, :]).then_inc(stored, 16)
                        if u == 0:
                            sp.dma_start(h2[:, 0, :], rows(h2_dram)[(U * i + U) % TILES]).then_inc(next_in, 16)
                            sp.wait_ge(stored, 16)
                            sp.dma_start(x1[:, 0, :], rows(x1_dram)[U * i + 2]).then_inc(x1_in[2], 16)
                    sp.wait_ge(next_in, 32)
                    sp.wait_ge(stored, 48)

                @block.gpsimd
                def _(pool):
                    for n in range(R, U * SLOTS):
                        if n % SLOTS == 0:
                            pool.wait_ge(chosen, CHOOSE * PEER_HEADS * (n // SLOTS))
                        pool.wait_ge(v_used, n - R + 1)
                        fetch(pool, n, n // SLOTS, n % SLOTS)
                    pool.wait_ge(chosen, CHOOSE * PEER_HEADS * U)
                    for r in range(R):
                        pool.wait_ge(v_used, U * SLOTS - R + r + 1)
                        fetch(pool, r, 0, r)
                    rest_fetches(pool, U * SLOTS // R)

                @block.tensor
                def _(pe):
                    for n in range(U * SLOTS):
                        u, k, h = n // SLOTS, n % SLOTS, n // TOPK
                        if n % TOPK == 0:
                            if k == 0 and u:
                                pe.wait_ge(h2T_in[(u + 1) % U], 16)
                            query_matmuls(pe, h, (u + 1) % U)
                        if n % TOPK == KEYS_AT:
                            key_matmuls(pe, h)
                        if k == 0 and u == 2:
                            pe.wait_ge(f_read, 2)
                        pe.wait_ge(diag_ready, n + 1)
                        for c in range(2):
                            last = pe.matmul(f[u % 2][c][:, :], diag[:, n % DG, :], ring[:, n % R, D + c * HALF:D + (c + 1) * HALF], start=(k == 0), stop=(k == SLOTS - 1))
                        last.then_inc(v_used, 1)

                @block.scalar
                def _(act):
                    def root(u):
                        act.wait_ge(normed, 6 * u + 5)
                        act.activation(rstd[:, :], rstd[:, :], ACT.Sqrt).then_inc(inverse, 1)

                    for j in range(U * GROUPS):
                        h, part = j * G // TOPK, j * G % TOPK
                        cols = slice(j % GROUPS * G, (j % GROUPS + 1) * G)
                        act.wait_ge(dot_done, (j + 1) * G)
                        act.activation(act_v[:, cols], dots[:, cols], ACT.Gelu_apprx_tanh).then_inc(gelu_done, 1)
                        if part == EXP_AT:
                            exp_best(act, h)
                        if j % GROUPS == END and j > GROUPS:
                            root(j // GROUPS - 1)
                        act.wait_ge(w_ready, j + 1)
                        for n in range(j * G, (j + 1) * G):
                            if n >= DG:
                                act.wait_ge(v_used, n - DG + 1)
                            act.activation(diag[:, n % DG, :], ident[:, :], ACT.Copy, scale=w[:, n % SLOTS:n % SLOTS + 1]).then_inc(diag_ready, 1)
                        if part == 0:
                            keep_query(act, h)
                        if part == KEYS_AT:
                            keep_scores(act, h)
                    root(U - 1)

                @block.vector
                def _(dve):
                    def weights(j):
                        cols = slice(j % GROUPS * G, (j % GROUPS + 1) * G)
                        dve.wait_ge(gelu_done, j + 1)
                        dve.tensor_tensor(w[:, cols], act_v[:, cols], gates[:, j // GROUPS, cols], ALU.mult).then_inc(w_ready, 1)

                    def end(u):
                        x, g, y = x1[:, u % 2, :], g2[:, u // 2, :], h2[:, u, :]
                        dve.wait_ge(v_used, SLOTS * (u + 1))
                        dve.wait_ge(dot_done, SLOTS * (u + 1))
                        if u == 2:
                            dve.wait_ge(gate2_in, 16)
                        for c in range(2):
                            cols = slice(c * HALF, (c + 1) * HALF)
                            dve.tensor_tensor(y[:, cols], f[u % 2][c][:, :], g[:, cols], ALU.mult).then_inc(f_read, 1)
                        dve.wait_ge(f_read, 2 * u + 2)
                        dve.wait_ge(x1_in[u], 16)
                        dve.scalar_tensor_tensor(x, x, ALPHA, y, ALU.mult, ALU.add).then_inc(ended, 1)
                        dve.wait_ge(ended, 3 * u + 1)
                        n = layer_norm_steps(dve, normed, inverse, u, 6 * u, x, stats[:, :, :], mv[:, :], rstd[:, :], x)
                        dve.wait_ge(normed, n)
                        dve.tensor_tensor(x, x, ln2[:, 0:D], ALU.mult).then_inc(ended, 1)
                        dve.wait_ge(ended, 3 * u + 2)
                        dve.tensor_tensor(x, x, ln2[:, D:2 * D], ALU.add).then_inc(ended, 1)

                    for j in range(U * GROUPS):
                        u, h, part = j // GROUPS, j * G // TOPK, j * G % TOPK
                        if u and j % GROUPS == 0:
                            dve.wait_ge(h2_in[u], 16)
                        for n in range(j * G, (j + 1) * G):
                            v = ring[:, n % R, 0:D]
                            if n >= R:
                                dve.wait_ge(ring_in[n % R], 16 * (n // R))
                            dve.scalar_tensor_tensor(v, v, 1.0, h2[:, u, :], ALU.mult, ALU.mult, accum_out=dots[:, n % SLOTS:n % SLOTS + 1]).then_inc(dot_done, 1)
                            if n % G == (G > 1) and j:
                                weights(j - 1)
                        if part == PARTS_AT:
                            choose_parts(dve, h)
                        if part == EXP_AT:
                            choose_best(dve, h, (u + 1) % U)
                        if j % GROUPS == END and u:
                            end(u - 1)
                    weights(U * GROUPS - 1)
                    end(U - 1)
            S.rest()


def laid_out(i):
    import numpy as np

    f = {k: np.asarray(v) for k, v in i.items()}
    one = {k: f[k][0] for k in ("w_ada", "b_ada", "w_in", "w_gla_gate", "b_gla_gate", "gla_norm_w", "w_gla_proj", "w_sb_proj", "w_o",
                                "ln1_w", "ln1_b", "peer_wq", "peer_keys", "peer_u", "peer_v", "ln2_w", "ln2_b")}

    def rows(w):
        return w.reshape(KC, P, -1).transpose(1, 0, 2)

    cols = np.cumsum([0, 512, 512, 1024, RANK, 1024, 1024, 1024, 1024, 1024, 1024])
    gq, gk, gv, glr, gog, sq, sk, sv, ma, mb = (one["w_in"][:, cols[n]:cols[n + 1]] for n in range(10))

    def padded(blocks):
        return np.concatenate([blocks, blocks[:1]])

    w_sb = padded(np.stack([np.stack([rows(m[:, p * P:(p + 1) * P]) for m in (sq, sk, sv)], 1) for p in range(SB_PAIRS)]))
    w_gla = padded(np.stack([np.concatenate([rows(gq[:, h * DK:(h + 1) * DK]), rows(gk[:, h * DK:(h + 1) * DK]),
                                             rows(gv[:, h * DV:(h + 1) * DV]), rows(gog[:, h * DV:(h + 1) * DV])], 2) for h in range(GLA_HEADS)]))
    w_mix = padded(np.stack([np.stack([rows(m[:, j * P:(j + 1) * P]) for m in (ma, mb, one["w_gla_proj"], one["w_sb_proj"])], 1) for j in range(KC)]))
    cache_k = f["cache_sb_k"][0].reshape(SEQS, PAST, SB_PAIRS, P)
    cache_v = f["cache_sb_v"][0].reshape(SEQS, PBLK, P, SB_PAIRS, P)

    at = np.arange(P)
    s_of, t_of = at // NEW, at % NEW
    q_s, q_t = np.repeat(np.arange(SEQS), 2 * NEW), np.tile(np.arange(NEW), 2 * SEQS)
    hide = np.float32(-1e30)
    tok = np.arange(TOK)
    goes_on = np.stack([np.where(tok < PROMPT, tok % P != 0, tok % NEW != 0), tok % SUB != 0]).astype(np.float32)
    sel = np.zeros((1 + SEQS, 2, P), np.float32)
    sel[0, 0, :] = 1
    sel[1 + s_of, 1, at] = 1
    return {
        "x": np.concatenate([f["x_prompt"].reshape(PROMPT, D), f["x_sample"].reshape(SEQS * NEW, D)]),
        "cT": np.concatenate([f["c_prompt"], f["c_sample"]]).T.reshape(KC, P, 1 + SEQS).transpose(1, 0, 2).reshape(P, -1),
        "w_ada": one["w_ada"], "b_ada": one["b_ada"][None],
        "w_sb": w_sb, "w_gla": w_gla, "w_mix": w_mix, "w_lr": rows(glr),
        "w_gate": one["w_gla_gate"], "b_gate": one["b_gla_gate"].reshape(GLA_HEADS, DK, 1),
        "gla_norm": one["gla_norm_w"][None],
        "w_o": rows(one["w_o"]), "w_q": rows(one["peer_wq"]),
        "keysT": one["peer_keys"].transpose(3, 0, 1, 2).reshape(P, PEER_HEADS * 2, NKEYS),
        "ln1": np.stack([one["ln1_w"], one["ln1_b"]]).reshape(1, 2 * D), "ln2": np.stack([one["ln2_w"], one["ln2_b"]]).reshape(1, 2 * D),
        "uv": np.concatenate([one["peer_u"], one["peer_v"]], 1),
        "kcT": cache_k.transpose(2, 3, 0, 1), "vc": cache_v.transpose(3, 2, 0, 1, 4),
        "s0": f["state_gla"][0].transpose(1, 2, 0, 3),
        "ident": np.eye(P, dtype=np.float32),
        "sel": sel,
        "from_here": (at[:, None] >= at[None]).astype(np.float32), "before": (at[:, None] < at[None]).astype(np.float32),
        "hide_diag": np.where(at[:, None] < at[None], 0, hide).astype(np.float32),
        "hide_self": np.where((s_of[:, None] == q_s[None]) & (t_of[:, None] < q_t[None]), 0, hide).astype(np.float32),
        "causal": np.stack([at[:, None] <= at[None], (at[:, None] <= at[None]) & (s_of[:, None] == s_of[None])], 1).astype(np.float32),
        "goes_on": goes_on,
        "own_rows": (s_of[:, None] == np.arange(SEQS)[None]).astype(np.float32),
        "sixteen": np.tile(np.arange(TOPK, dtype=np.float32), (P, 1)),
    }

def stream_layer_kernel(nc, A, y, kout, vout, prompt_state, sample_state):
    def dram(name, shape):
        return nc.dram_tensor(name, shape, F32, kind="Internal").ap()

    modb = dram("modb", [2, P, MODS])
    oA, oB, mixT = (dram(n, [KC, P, TOK]) for n in ("oA", "oB", "mixT"))
    x1, h2, h2T = dram("x1", [TOK, D]), dram("h2", [TOK, D]), dram("h2T", [TILES, P, D])
    mods_phase(nc, A, modb)
    with nc.sbuf_tensor("hT", [P, KC, TOK], F32) as hT:
        norm_phase(nc, A, modb, hT)
        stick_phase(nc, A, hT, oB, kout, vout)
        gla_phase(nc, A, hT, oA, prompt_state, sample_state)
        mix_phase(nc, A, hT, oA, oB, mixT)
    residual_phase(nc, A, modb, mixT, x1, h2, h2T)
    peer_phase(nc, A, modb, x1, h2, h2T, y)


def kernel(**inputs):
    import numpy as np
    import concourse.bacc as bacc
    from concourse.bass_utils import run_bass_kernel_spmd as run

    nc = bacc.Bacc("TRN2", target_bir_lowering=False, num_devices=1)
    arrays, A = {}, {}
    for name, a in laid_out(inputs).items():
        arrays["in_" + name] = np.ascontiguousarray(a)
        A[name] = nc.dram_tensor("in_" + name, a.shape, mybir.dt.from_np(a.dtype), kind="ExternalInput").ap()
    shapes = {"y": [TOK, D], "k": [TOK, D], "v": [TOK, D], "prompt_state": [GLA_HEADS, DK, DV], "sample_state": [GLA_HEADS, DK, SEQS, DV]}
    outs = [nc.dram_tensor("out_" + name, shape, F32, kind="ExternalOutput").ap() for name, shape in shapes.items()]
    stream_layer_kernel(nc, A, *outs)
    got = run(nc, [arrays], core_ids=[0]).results[0]
    y, k, v, prompt_state, sample_state = (got["out_" + name] for name in shapes)
    heads = (2 * SB_PAIRS, HD)
    return (y[:PROMPT].reshape(1, PROMPT, D), y[PROMPT:].reshape(SEQS, NEW, D),
            prompt_state[None, None], k[:PROMPT].reshape(1, 1, PROMPT, *heads), v[:PROMPT].reshape(1, 1, PROMPT, *heads),
            sample_state.transpose(2, 0, 1, 3)[None], k[PROMPT:].reshape(1, SEQS, NEW, *heads), v[PROMPT:].reshape(1, SEQS, NEW, *heads))
```

```python
from contextlib import ExitStack

import concourse.bass as bass
from concourse import mybir

F32 = mybir.dt.float32
BF16 = mybir.dt.bfloat16
U32 = mybir.dt.uint32
F32R = mybir.dt.float32r
ALU = mybir.AluOpType
ACT = mybir.ActivationFunctionType
AX_X = mybir.AxisListType.X

P = 128
D = 1024
KC = D // P
PROMPT = 1024
SEQS, NEW = 8, 16
TOK = PROMPT + SEQS * NEW
TILES = TOK // P
PTILES = PROMPT // P
PAST = 1024
PBLK = PAST // P
HALF = 512
MODS = 6 * D
SB_PAIRS, HD = 8, 64
GLA_HEADS, DK, DV = 4, 128, 256
SUB = 16
SUBS = P // SUB
RANK = 16
PEER_HEADS, NKEYS, TOPK = 8, 128, 16
CHUNK = 384
CHUNKS = TOK // CHUNK
LN_EPS, RMS_EPS = 1e-5, 1e-6
ALPHA = 2.0 ** 0.25
TAU = 16.0
NEG = -3.0e38


class Scope:

    def __init__(self, nc, ctx, tag):
        self.nc, self.ctx, self.tag, self.sems = nc, ctx, tag, []

    def sb(self, name, shape, dt=F32):
        return self.ctx.enter_context(self.nc.sbuf_tensor(f"{self.tag}_{name}", shape, dt))

    def ps(self, name, shape, dt=F32):
        return self.ctx.enter_context(self.nc.psum_tensor(f"{self.tag}_{name}", shape, dt))

    def sem(self, name):
        s = self.ctx.enter_context(self.nc.semaphore(f"{self.tag}_{name}"))
        self.sems.append(s)
        return s

    def rest(self):
        nums = sorted(s.num for s in self.sems)
        first = nums[0]
        for n in nums:
            if n + 1 not in nums:
                self.nc.all_engine_barrier(sems_to_clear=range(first, n + 1))
                first = min((m for m in nums if m > n), default=None)


def layer_norm_steps(e, done, inverse, turn, n, x, stats, mv, rstd, out):
    for c in range(2):
        e.bn_stats(stats[:, c, :], x[:, c * HALF:(c + 1) * HALF]).then_inc(done, 1)
    e.wait_ge(done, n + 2)
    e.bn_aggr(mv, stats).then_inc(done, 1)
    e.wait_ge(done, n + 3)
    e.tensor_scalar(rstd, mv[:, 1:2], LN_EPS, None, ALU.add).then_inc(done, 1)
    e.wait_ge(done, n + 4)
    e.reciprocal(rstd, rstd).then_inc(done, 1)
    e.wait_ge(inverse, turn + 1)
    e.tensor_scalar(out, x, mv[:, 0:1], rstd, ALU.subtract, ALU.mult).then_inc(done, 1)
    return n + 6


def mods_phase(nc, A, modb):
    BLK = MODS // HALF
    RING = 3
    with ExitStack() as ctx:
        S = Scope(nc, ctx, "mod")
        c_sb, silu_c = S.sb("c", [P, KC * (1 + SEQS)]), S.sb("silu", [P, KC * (1 + SEQS)])
        bias, ones = S.sb("bias", [1, MODS]), S.sb("ones", [1, 1 + SEQS])
        sel = S.sb("sel", [1 + SEQS, 2, P])
        w = S.sb("w", [P, RING, KC, HALF])
        mod = S.sb("mod", [1 + SEQS, MODS])
        spread = S.sb("spread", [P, 2, MODS])
        acc = [S.ps(f"acc{i}", [1 + SEQS, HALF]) for i in range(2)]
        rows = [S.ps(f"rows{i}", [P, HALF]) for i in range(2)]
        small_in, bias_in, sel_in = S.sem("small_in"), S.sem("bias_in"), S.sem("sel_in")
        w_in = [S.sem(f"w_in{i}") for i in range(RING)]
        ones_set, silu_done, acc_full, mod_kept = S.sem("ones"), S.sem("silu"), S.sem("acc_full"), S.sem("mod_kept")
        rows_full, rows_kept, stored = S.sem("rows_full"), S.sem("rows_kept"), S.sem("stored")
        with nc.Block() as block:

            @block.sync
            def _(sp):
                sp.dma_start(c_sb[:, :], A["cT"]).then_inc(small_in, 16)
                for j in range(BLK):
                    if j >= RING:
                        sp.wait_ge(acc_full, j - RING + 1)
                    sp.dma_start(w[:, j % RING], A["w_ada"].rearrange("(k p) n -> p k n", p=P)[:, :, j * HALF:(j + 1) * HALF]).then_inc(w_in[j % RING], 16)
                sp.wait_ge(rows_kept, 2 * BLK)
                sp.dma_start(modb.rearrange("g p n -> p g n"), spread[:, :, :]).then_inc(stored, 16)
                sp.wait_ge(stored, 16)

            @block.scalar
            def _(act):
                act.dma_start(bias[:, :], A["b_ada"]).then_inc(bias_in, 16)
                act.dma_start(sel[:, :, :], A["sel"]).then_inc(sel_in, 16)
                act.wait_ge(small_in, 16)
                act.activation(silu_c[:, :], c_sb[:, :], ACT.Silu).then_inc(silu_done, 1)
                for n in range(2 * BLK):
                    j, g = n // 2, n % 2
                    act.wait_ge(rows_full, n + 1)
                    act.activation(spread[:, g, j * HALF:(j + 1) * HALF], rows[n % 2][:, :], ACT.Copy).then_inc(rows_kept, 1)

            @block.tensor
            def _(pe):
                pe.wait_ge(silu_done, 1)
                pe.wait_ge(bias_in, 16)
                pe.wait_ge(ones_set, 1)
                for j in range(BLK):
                    if j >= 2:
                        pe.wait_ge(mod_kept, j - 1)
                    pe.wait_ge(w_in[j % RING], 16 * (j // RING + 1))
                    for k in range(KC):
                        pe.matmul(acc[j % 2][:, :], silu_c[:, k * (1 + SEQS):(k + 1) * (1 + SEQS)], w[:, j % RING, k, :], start=(k == 0), stop=False)
                    pe.matmul(acc[j % 2][:, :], ones[0:1, :], bias[0:1, j * HALF:(j + 1) * HALF], start=False, stop=True).then_inc(acc_full, 1)
                pe.wait_ge(sel_in, 16)
                for n in range(2 * BLK):
                    j, g = n // 2, n % 2
                    pe.wait_ge(mod_kept, j + 1)
                    if n >= 2:
                        pe.wait_ge(rows_kept, n - 1)
                    pe.matmul(rows[n % 2][:, :], sel[:, g, :], mod[:, j * HALF:(j + 1) * HALF], start=True, stop=True).then_inc(rows_full, 1)

            @block.vector
            def _(dve):
                dve.memset(ones[:, :], 1.0).then_inc(ones_set, 1)
                for j in range(BLK):
                    dve.wait_ge(acc_full, j + 1)
                    dve.tensor_copy(mod[:, j * HALF:(j + 1) * HALF], acc[j % 2][:, :]).then_inc(mod_kept, 1)
        S.rest()


def norm_phase(nc, A, modb, hT):
    U = 3
    with ExitStack() as ctx:
        S = Scope(nc, ctx, "norm")
        ident = S.sb("ident", [P, P])
        x = S.sb("x", [P, U, D])
        xn = S.sb("xn", [P, U, D])
        h = S.sb("h", [P, U, D])
        mods = S.sb("mods", [P, 2, 2 * D])
        stats, mv, rstd = S.sb("stats", [P, U, 2, 6]), S.sb("mv", [P, U, 2]), S.sb("rstd", [P, U])
        turned = [S.ps(f"turned{i}", [P, 4, P]) for i in range(2)]
        ident_in, x_in, mods_in = S.sem("ident_in"), [S.sem(f"x_in{u}") for u in range(U)], [S.sem(f"mods_in{g}") for g in range(2)]
        inverse = S.sem("inverse")
        normed, h_ready, turned_full, hT_kept = S.sem("normed"), S.sem("h_ready"), S.sem("turned_full"), S.sem("hT_kept")
        with nc.Fori(0, TILES // U) as i:
            with nc.Block() as block:

                @block.sync
                def _(sp):
                    for u in range(U):
                        sp.dma_start(x[:, u, :], A["x"].rearrange("(t p) n -> t p n", p=P)[U * i + u]).then_inc(x_in[u], 16)
                    sp.dma_start(ident[:, :], A["ident"]).then_inc(ident_in, 16)

                @block.scalar
                def _(act):
                    act.dma_start(mods[:, 0, :], modb[0, :, 0:2 * D]).then_inc(mods_in[0], 16)
                    act.dma_start(mods[:, 1, :], modb[i // 2, :, 0:2 * D]).then_inc(mods_in[1], 16)
                    for u in range(U):
                        act.wait_ge(normed, 6 * u + 5)
                        act.activation(rstd[:, u:u + 1], rstd[:, u:u + 1], ACT.Sqrt).then_inc(inverse, 1)
                    for n in range(2 * U):
                        u, c = n // 2, n % 2
                        act.wait_ge(turned_full, n + 1)
                        act.activation(hT[:, 4 * c:4 * c + 4, bass.ds(U * P * i + P * u, P)], turned[n % 2][:, :, :], ACT.Copy).then_inc(hT_kept, 1)

                @block.tensor
                def _(pe):
                    pe.wait_ge(ident_in, 16)
                    for n in range(2 * U):
                        u, c = n // 2, n % 2
                        pe.wait_ge(h_ready, 2 * u + 2)
                        if n >= 2:
                            pe.wait_ge(hT_kept, n - 1)
                        for k in range(4):
                            last = pe.transpose(turned[n % 2][:, k, :], h[:, u, (4 * c + k) * P:(4 * c + k + 1) * P], ident[:, :])
                        last.then_inc(turned_full, 1)

                @block.vector
                def _(dve):
                    n = 0
                    for u in range(U):
                        dve.wait_ge(x_in[u], 16)
                        n = layer_norm_steps(dve, normed, inverse, u, n, x[:, u, :], stats[:, u], mv[:, u], rstd[:, u:u + 1], xn[:, u, :])
                        dve.wait_ge(normed, n)
                        dve.wait_ge(mods_in[u // 2], 16)
                        m = mods[:, u // 2, :]
                        dve.scalar_tensor_tensor(h[:, u, :], m[:, D:2 * D], 1.0, xn[:, u, :], ALU.add, ALU.mult).then_inc(h_ready, 1)
                        dve.wait_ge(h_ready, 2 * u + 1)
                        dve.tensor_tensor(h[:, u, :], h[:, u, :], m[:, 0:D], ALU.add).then_inc(h_ready, 1)
            S.rest()


def stick_phase(nc, A, hT, oB_dram, kout, vout):
    SC = SEQS * 2 * NEW
    with ExitStack() as ctx:
        S = Scope(nc, ctx, "sb")
        ident, identb = S.sb("ident", [P, P]), S.sb("identb", [P, P], BF16)
        ones = S.sb("ones", [P, 2, P], F32R)
        hide_diag, hide_self = S.sb("hide_diag", [P, P], BF16), S.sb("hide_self", [P, SC], BF16)
        w = S.sb("w", [P, 3, KC, P])
        qT, kT = S.sb("qT", [P, TOK]), S.sb("kT", [P, TOK])
        v, kn = S.sb("v", [P, TILES, P]), S.sb("kn", [P, TILES, P])
        kc, vc = S.sb("kc", [P, SEQS, PAST]), S.sb("vc", [P, SEQS, PBLK, P])
        qd = S.sb("qd", [P, SEQS, 2, NEW])
        oB = qT
        k_parts = S.sb("k_parts", [P, 2, PROMPT], F32R)
        q_high, q_low = S.sb("q_high", [P, 2, PROMPT], F32R), S.sb("q_low", [P, 2, PROMPT], F32R)
        NZ, NT, NH, NA = 6, 4, 4, 3
        zs, t, a = S.sb("zs", [P, NZ, HALF]), S.sb("t", [P, NT, HALF]), S.sb("a", [P, NA, HALF])
        high, low = S.sb("high", [P, NH, HALF], F32R), S.sb("low", [P, NH, HALF], F32R)
        banks = [S.ps(f"bank{i}", [P, HALF]) for i in range(8)]
        zb = banks[0:2]
        rest = dict(X=banks[2], Y=banks[3], C=banks[4])
        o_late, o_early, o_new = banks[5], banks[6], banks[7]

        const_in, w_in = S.sem("const_in"), S.sem("w_in")
        zeros_set = S.sem("zeros_set")
        kc_in, vc_in = S.sem("kc_in"), S.sem("vc_in")
        proj_full, q_kept, k_kept, v_kept, kn_kept, qd_set = (S.sem(n) for n in ("proj_full", "q_kept", "k_kept", "v_kept", "kn_kept", "qd_set"))
        kn_full, highs, lows, k_lows = S.sem("kn_full"), S.sem("highs"), S.sem("lows"), S.sem("k_lows")
        high_ready, low_ready = S.sem("high_ready"), S.sem("low_ready")
        z_full, t_capped, t_exp, t_log, sp_ready = (S.sem(n) for n in ("z_full", "t_capped", "t_exp", "t_log", "sp_ready"))
        z_kept = [S.sem(f"z_kept_by_{n}") for n in ("act", "dve")]
        rest_full, e_ready, a_ready, rest_added, o_added = (S.sem(n) for n in ("rest_full", "e_ready", "a_ready", "rest_added", "o_added"))
        o_kept, stored = S.sem("o_kept"), S.sem("stored")

        with nc.Block() as block:

            @block.sync
            def _(sp):
                sp.dma_start(ident[:, :], A["ident"]).then_inc(const_in, 16)
                sp.dma_start(zs[:, 2, 0:P], A["from_here"]).then_inc(const_in, 16)
                sp.dma_start(zs[:, 3, 0:P], A["before"]).then_inc(const_in, 16)
                sp.dma_start(w[:, :, :, :], A["w_sb"][0]).then_inc(w_in, 16)
                sp.wait_ge(w_in, 16)
                sp.wait_ge(const_in, 16 * 5)

            @block.scalar
            def _(act):
                act.dma_start(zs[:, 0, 0:P], A["hide_diag"]).then_inc(const_in, 16)
                act.dma_start(zs[:, 1, 0:SC], A["hide_self"]).then_inc(const_in, 16)

            @block.vector
            def _(dve):
                dve.memset(qd[:, :, :, :], 0.0).then_inc(zeros_set, 1)
                dve.wait_ge(const_in, 16 * 5)
                dve.tensor_copy(identb[:, :], ident[:, :]).then_inc(zeros_set, 1)
                dve.tensor_copy(hide_diag[:, :], zs[:, 0, 0:P]).then_inc(zeros_set, 1)
                dve.tensor_copy(hide_self[:, :], zs[:, 1, 0:SC]).then_inc(zeros_set, 1)
                for n in range(2):
                    dve.tensor_copy(ones[:, n, :], zs[:, 2 + n, 0:P]).then_inc(zeros_set, 1)
                dve.wait_ge(zeros_set, 6)
        S.rest()

        X = [("X", 0, g, kb) for g in (1, 0) for kb in range(4 * g + 3, -1, -1)]
        Y = [("Y", 1, g, kb) for g in (1, 0) for kb in range(4 * g + 3, -1, -1)]
        C = [("C", None, None, kb) for kb in [None] + list(range(PBLK - 1, -1, -1))]
        steps = []
        for n in range(max(len(X), len(C))):
            steps += [c[n] for c in (X, Y, C) if n < len(c)]
        N = len(steps)

        def first_col(step):
            _, head, g, kb = step
            return 0 if head is None else max(0, kb - 4 * g) * P

        def width(step):
            return SC if step[1] is None else HALF

        def chain_start(step):
            _, head, g, kb = step
            return kb is None if head is None else kb == 4 * g + 3

        def last_step(chain, g=None):
            return max(n for n, s in enumerate(steps) if s[0] == chain and s[2] == g) + 1

        KEEP, LOG, SOFTPLUS, HERE, EXPONENT, LATER, WEIGHTS, VALUES = 1, 2, 3, 4, 5, 6, 6, 7

        def adds_rest(step):
            return step[3] != 0

        def rests_added(n):
            return sum(adds_rest(s) for s in steps[:n + 1])

        def kept_by_act(n):
            return n % 2 == 0

        late_whole = max(last_step("X", 1), last_step("Y", 1))
        early_whole = max(last_step("X", 0), last_step("Y", 0))
        new_whole = last_step("C")

        with nc.Fori(0, SB_PAIRS) as pair:
            with nc.Block() as block:

                @block.sync
                def _(sp):
                    sp.dma_start(kc[:, :, :], A["kcT"][pair]).then_inc(kc_in, 16)
                    sp.dma_start(vc[:, :, :, :], A["vc"][pair]).then_inc(vc_in, 16)
                    sp.wait_ge(proj_full, 9)
                    sp.dma_start(w[:, :, :, :], A["w_sb"][pair + 1]).then_inc(w_in, 16)
                    sp.wait_ge(kn_kept, 3)
                    sp.dma_start(kout.rearrange("(t p) n -> p t n", p=P)[:, :, bass.ds(pair * P, P)], kn[:, :, :]).then_inc(stored, 16)
                    sp.wait_ge(v_kept, 3)
                    sp.dma_start(vout.rearrange("(t p) n -> p t n", p=P)[:, :, bass.ds(pair * P, P)], v[:, :, :]).then_inc(stored, 16)
                    sp.wait_ge(o_kept, 4)
                    sp.dma_start(oB_dram[pair], oB[:, :]).then_inc(stored, 16)
                    sp.wait_ge(w_in, 16)
                    sp.wait_ge(stored, 48)

                @block.tensor
                def _(pe):
                    for g in range(9):
                        bank = banks[g % 8]
                        if g == 8:
                            pe.wait_ge(q_kept, 1)
                        if g < 6:
                            c = g % 3
                            for k in range(KC):
                                last = pe.matmul(bank[:, 0:CHUNK], w[:, g // 3, k, :], hT[:, k, c * CHUNK:(c + 1) * CHUNK], start=(k == 0), stop=(k == KC - 1))
                        else:
                            for u in range(3):
                                tile = 3 * (g - 6) + u
                                for k in range(KC):
                                    last = pe.matmul(bank[:, u * P:(u + 1) * P], hT[:, k, tile * P:(tile + 1) * P], w[:, 2, k, :], start=(k == 0), stop=(k == KC - 1))
                        last.then_inc(proj_full, 1)
                    for g in range(3):
                        pe.wait_ge(k_kept, g + 1)
                        pe.wait_ge(q_kept, 3)
                        pe.wait_ge(v_kept, 3)
                        for u in range(3):
                            tile = 3 * g + u
                            last = pe.transpose(banks[1 + g][:, u * P:(u + 1) * P], kT[:, tile * P:(tile + 1) * P], ident[:, :])
                        last.then_inc(kn_full, 1)
                    pe.wait_ge(kn_kept, 3)
                    pe.wait_ge(qd_set, 2)
                    pe.wait_ge(highs, 6)
                    pe.wait_ge(lows, 4)
                    pe.wait_ge(k_lows, 2)

                    def scores(n):
                        step = steps[n]
                        _, head, g, kb = step
                        if n >= 2:
                            by = z_kept[n % 2]
                            pe.wait_ge(by, n // 2)
                        out = zb[n % 2]
                        if head is None and kb is None:
                            pe.matmul(out[:, 0:SC], kT[:, PROMPT:TOK], qd[:, :, :, :].rearrange("p s h t -> p (s h t)"), start=True, stop=False)
                            last = pe.matmul(out[:, 0:SC], identb[:, :], hide_self[:, :], start=False, stop=True)
                        elif head is None:
                            if kb == PBLK - 1:
                                pe.wait_ge(kc_in, 16)
                            for s in range(SEQS):
                                last = pe.matmul(out[:, s * 2 * NEW:(s + 1) * 2 * NEW], kc[:, s, kb * P:(kb + 1) * P],
                                                 qd[:, s].rearrange("p h t -> p (h t)"), start=True, stop=True)
                        else:
                            c0 = first_col(step)
                            diagonal = kb >= 4 * g
                            for q in (q_high, q_low):
                                last = pe.matmul(out[:, c0:HALF], k_parts[:, head, kb * P:(kb + 1) * P], q[:, head, g * HALF + c0:(g + 1) * HALF],
                                                 start=(q is q_high), stop=(q is q_low and not diagonal))
                            if diagonal:
                                last = pe.matmul(out[:, c0:c0 + P], identb[:, :], hide_diag[:, :], start=False, stop=True)
                        last.then_inc(z_full, 1)

                    def to_here(n):
                        step = steps[n]
                        chain, head, g, kb = step
                        bank = rest[chain]
                        c0, c1 = first_col(step), width(step)
                        pe.wait_ge(high_ready, n + 1)
                        pe.matmul(bank[:, c0:c1], ones[:, 0, :], high[:, n % NH, c0:c1], start=chain_start(step), stop=True, skip_group_check=True)
                        pe.wait_ge(low_ready, n + 1)
                        pe.matmul(bank[:, c0:c1], ones[:, 0, :], low[:, n % NH, c0:c1], start=False, stop=True, skip_group_check=True).then_inc(rest_full, 1)

                    def later_keys(n):
                        step = steps[n]
                        c0, c1 = first_col(step), width(step)
                        pe.wait_ge(e_ready, n + 1)
                        for part in (high, low):
                            last = pe.matmul(rest[step[0]][:, c0:c1], ones[:, 1, :], part[:, n % NH, c0:c1], start=False, stop=True, skip_group_check=True)
                        last.then_inc(rest_added, 1)

                    def values(n):
                        step = steps[n]
                        chain, head, g, kb = step
                        c0, c1 = first_col(step), width(step)
                        pe.wait_ge(a_ready, n + 1)
                        if head is None:
                            if kb is None:
                                last = pe.matmul(o_new[:, 0:SC], v[:, TILES - 1, :], a[:, n % NA, 0:SC], start=True, stop=False)
                            else:
                                if kb == PBLK - 1:
                                    pe.wait_ge(vc_in, 16)
                                for s in range(SEQS):
                                    cols = slice(s * 2 * NEW, (s + 1) * 2 * NEW)
                                    last = pe.matmul(o_new[:, cols], vc[:, s, kb, :], a[:, n % NA, cols], start=False, stop=(kb == 0 and s == SEQS - 1))
                        else:
                            out = (o_late if g == 1 else o_early)[head * HD:(head + 1) * HD, :]
                            last = pe.matmul(out[:, c0:HALF], v[:, kb, head * HD:(head + 1) * HD], a[:, n % NA, c0:HALF], start=chain_start(step), stop=(kb == 0), skip_group_check=True)
                        last.then_inc(o_added, 1)

                    for s in range(N + VALUES):
                        if s < N:
                            scores(s)
                        if 0 <= s - LATER < N and adds_rest(steps[s - LATER]):
                            later_keys(s - LATER)
                        if 0 <= s - HERE < N:
                            to_here(s - HERE)
                        if 0 <= s - VALUES < N:
                            values(s - VALUES)

                @block.scalar
                def _(act):
                    act.preload_act_table_set("natural_log_exp_and_others")
                    for c in range(3):
                        act.wait_ge(proj_full, c + 1)
                        act.activation(qT[:, c * CHUNK:(c + 1) * CHUNK], banks[c][:, 0:CHUNK], ACT.Copy, scale=HD ** -0.5).then_inc(q_kept, 1)
                    act.wait_ge(q_kept, 3)
                    for hh in range(2):
                        rows = slice(hh * HD, (hh + 1) * HD)
                        act.activation(qd[rows, :, hh, :], qT[rows, PROMPT:TOK].rearrange("p (s t) -> p s t", t=NEW), ACT.Copy).then_inc(qd_set, 1)
                    for g in range(3):
                        act.wait_ge(proj_full, 7 + g)
                        act.activation(v[:, 3 * g:3 * g + 3, :].rearrange("p t n -> p (t n)"), banks[(6 + g) % 8][:, 0:CHUNK], ACT.Copy).then_inc(v_kept, 1)

                    def keep(n):
                        c0, c1 = first_col(steps[n]), width(steps[n])
                        act.wait_ge(z_full, n + 1)
                        if n >= NZ:
                            act.wait_ge(a_ready, n - NZ + 1)
                        act.activation(zs[:, n % NZ, c0:c1], zb[n % 2][:, c0:c1], ACT.Copy).then_inc(z_kept[0], 1)

                    def exp_log(n):
                        c0, c1 = first_col(steps[n]), width(steps[n])
                        act.wait_ge(t_capped, n + 1)
                        act.activation(t[:, n % NT, c0:c1], t[:, n % NT, c0:c1], ACT.Exp).then_inc(t_exp, 1)
                        act.wait_ge(t_exp, n + 1)
                        act.activation(t[:, n % NT, c0:c1], t[:, n % NT, c0:c1], ACT.Ln, bias=1.0).then_inc(t_log, 1)

                    def weights(n):
                        c0, c1 = first_col(steps[n]), width(steps[n])
                        act.wait_ge(e_ready, n + 1)
                        if n >= NA:
                            act.wait_ge(o_added, n - NA + 1)
                        act.activation(a[:, n % NA, c0:c1], zs[:, n % NZ, c0:c1], ACT.Exp).then_inc(a_ready, 1)

                    for s in range(N + WEIGHTS):
                        if 0 <= s - KEEP < N and kept_by_act(s - KEEP):
                            keep(s - KEEP)
                        if 0 <= s - LOG < N:
                            exp_log(s - LOG)
                        if 0 <= s - WEIGHTS < N:
                            weights(s - WEIGHTS)

                @block.gpsimd
                def _(pool):
                    for hh in range(2):
                        rows = slice(hh * HD, (hh + 1) * HD)
                        pool.wait_ge(highs, 3 * hh + 2)
                        for dst in (q_low[0:HD, hh, :], q_low[HD:P, hh, :]):
                            pool.tensor_tensor(dst, qT[rows, 0:PROMPT], q_high[rows, hh, :].bitcast(F32), ALU.subtract).then_inc(lows, 1)
                    for n in range(N):
                        c0, c1 = first_col(steps[n]), width(steps[n])
                        pool.wait_ge(high_ready, n + 1)
                        if n >= NH:
                            pool.wait_ge(rest_added, rests_added(n - NH))
                            pool.wait_ge(rest_full, n - NH + 1)
                        pool.tensor_tensor(low[:, n % NH, c0:c1], t[:, n % NT, c0:c1], high[:, n % NH, c0:c1].bitcast(F32), ALU.subtract).then_inc(low_ready, 1)

                @block.vector
                def _(dve):
                    for c in range(3):
                        dve.wait_ge(proj_full, 4 + c)
                        dve.tensor_copy(kT[:, c * CHUNK:(c + 1) * CHUNK], banks[3 + c][:, 0:CHUNK]).then_inc(k_kept, 1)
                    dve.wait_ge(k_kept, 3)
                    dve.wait_ge(q_kept, 3)
                    for hh in range(2):
                        rows = slice(hh * HD, (hh + 1) * HD)
                        for dst in (q_high[0:HD, hh, :], q_high[HD:P, hh, :]):
                            dve.tensor_copy(dst, qT[rows, 0:PROMPT]).then_inc(highs, 1)
                        dve.tensor_copy(k_parts[rows, hh, :], kT[rows, 0:PROMPT]).then_inc(highs, 1)
                        dve.wait_ge(highs, 3 * hh + 3)
                        dve.tensor_tensor(k_parts[(1 - hh) * HD:(2 - hh) * HD, hh, :], kT[rows, 0:PROMPT], k_parts[rows, hh, :].bitcast(F32), ALU.subtract).then_inc(k_lows, 1)
                    for g in range(3):
                        dve.wait_ge(kn_full, g + 1)
                        dve.tensor_copy(kn[:, 3 * g:3 * g + 3, :].rearrange("p t n -> p (t n)"), banks[1 + g][:, 0:CHUNK]).then_inc(kn_kept, 1)

                    def keep(n):
                        c0, c1 = first_col(steps[n]), width(steps[n])
                        dve.wait_ge(z_full, n + 1)
                        if n >= NZ:
                            dve.wait_ge(a_ready, n - NZ + 1)
                        dve.tensor_copy(zs[:, n % NZ, c0:c1], zb[n % 2][:, c0:c1]).then_inc(z_kept[1], 1)

                    def capped(n):
                        c0, c1 = first_col(steps[n]), width(steps[n])
                        dve.wait_ge(z_kept[n % 2], n // 2 + 1)
                        if n >= NT:
                            dve.wait_ge(low_ready, n - NT + 1)
                        dve.tensor_scalar(t[:, n % NT, c0:c1], zs[:, n % NZ, c0:c1], 20.0, None, ALU.min).then_inc(t_capped, 1)

                    def softplus(n):
                        c0, c1 = first_col(steps[n]), width(steps[n])
                        dve.wait_ge(t_log, n + 1)
                        dve.tensor_tensor(t[:, n % NT, c0:c1], zs[:, n % NZ, c0:c1], t[:, n % NT, c0:c1], ALU.max).then_inc(sp_ready, 1)
                        dve.wait_ge(sp_ready, n + 1)
                        if n >= NH:
                            dve.wait_ge(rest_added, rests_added(n - NH))
                            dve.wait_ge(rest_full, n - NH + 1)
                        dve.tensor_copy(high[:, n % NH, c0:c1], t[:, n % NT, c0:c1]).then_inc(high_ready, 1)

                    def exponent(n):
                        c0, c1 = first_col(steps[n]), width(steps[n])
                        dve.wait_ge(rest_full, n + 1)
                        dve.wait_ge(sp_ready, n + 1)
                        dve.tensor_tensor(zs[:, n % NZ, c0:c1], zs[:, n % NZ, c0:c1], rest[steps[n][0]][:, c0:c1], ALU.subtract).then_inc(e_ready, 1)

                    for s in range(N + EXPONENT):
                        if 0 <= s - KEEP < N:
                            if not kept_by_act(s - KEEP):
                                keep(s - KEEP)
                            capped(s - KEEP)
                        if 0 <= s - SOFTPLUS < N:
                            softplus(s - SOFTPLUS)
                        if 0 <= s - EXPONENT < N:
                            exponent(s - EXPONENT)
                    dve.wait_ge(o_added, early_whole)
                    dve.wait_ge(o_added, late_whole)
                    dve.wait_ge(o_added, new_whole)
                    dve.tensor_copy(oB[:, HALF:PROMPT], o_late[:, :]).then_inc(o_kept, 1)
                    dve.tensor_copy(oB[:, 0:HALF], o_early[:, :]).then_inc(o_kept, 1)
                    for hh in range(2):
                        rows = slice(hh * HD, (hh + 1) * HD)
                        dve.tensor_copy(oB[rows, PROMPT:TOK].rearrange("p (s t) -> p s t", t=NEW),
                                        o_new[rows, 0:SC].rearrange("p (s h t) -> p s h t", s=SEQS, h=2)[:, :, hh, :]).then_inc(o_kept, 1)
            S.rest()


def gla_phase(nc, A, hT, oA_dram, prompt_state, sample_state):
    with ExitStack() as ctx:
        S = Scope(nc, ctx, "gla")
        ident = S.sb("ident", [P, P])
        causal = S.sb("causal", [P, 2, P])
        goes_on = S.sb("goes_on", [P, 2, TOK])
        own_rows = S.sb("own_rows", [P, SEQS])
        norm_w = S.sb("norm_w", [P, DV])
        w_lr, lrT = S.sb("w_lr", [P, KC, RANK]), S.sb("lrT", [RANK, TOK])
        w = S.sb("w", [P, KC, 2 * DK + 2 * DV])
        w_gate, b_gate = S.sb("w_gate", [RANK, DK]), S.sb("b_gate", [P, 1])
        qT, kT, la, b, c = (S.sb(n, [P, TOK]) for n in ("qT", "kT", "la", "b", "c"))
        eb, ec, kd = (S.sb(n, [P, TOK]) for n in ("eb", "ec", "kd"))
        v, og, o_raw = S.sb("v", [P, TILES, DV]), S.sb("og", [P, TILES, DV]), S.sb("o_raw", [P, TILES, DV])
        KL = 3
        kl = S.sb("kl", [P, KL, SUBS, P])
        att = S.sb("att", [P, 2, P])
        kdn = S.sb("kdn", [P, 2, P])
        state = S.sb("state", [P, 2, DV])
        s0 = S.sb("s0", [P, SEQS, DV])
        v_own = S.sb("v_own", [P, SEQS, DV])
        q_own = S.sb("q_own", [P, SEQS * (P + NEW)])
        decay = S.sb("decay", [P, PTILES + SEQS])
        squares, rms, junk = S.sb("squares", [P, TILES]), S.sb("rms", [P, TILES]), S.sb("junk", [P, DV])
        oT = S.sb("oT", [P, 2, TOK])
        banks = [S.ps(f"bank{i}", [P, HALF]) for i in range(8)]

        const_in, w_in, lr_full, zeroed, gate_in, s0_in, proj_full, act_kept = (S.sem(n) for n in ("const_in", "w_in", "lr_full", "zeroed", "gate_in", "s0_in", "proj_full", "act_kept"))
        dve_kept, capped, gate_exp, gate_log, la_min, la_ready, b_ready, c_ready = (S.sem(n) for n in ("dve_kept", "capped", "gate_exp", "gate_log", "la_min", "la_ready", "b_ready", "c_ready"))
        eb_ready, ec_ready, decays, kd_diff, kd_exp, products, og_scaled, kl_exp = (S.sem(n) for n in ("eb_ready", "ec_ready", "decays", "kd_diff", "kd_exp", "products", "og_scaled", "kl_exp"))
        kl_ready, att_full, att_ready, kdT_full, kdn_ready, o_full, u_full, state_ready = (S.sem(n) for n in ("kl_ready", "att_full", "att_ready", "kdT_full", "kdn_ready", "o_full", "u_full", "state_ready"))
        o_kept, squared, v_split, q_split, s0_ready, mean_sq, mean_inv, root = (S.sem(n) for n in ("o_kept", "squared", "v_split", "q_split", "s0_ready", "mean_sq", "mean_inv", "root"))
        o_normed, oT_full, oT_kept, stored = (S.sem(n) for n in ("o_normed", "oT_full", "oT_kept", "stored"))
        og_full, og_kept, og_silu = (S.sem(n) for n in ("og_full", "og_kept", "og_silu"))
        kept = {"act_kept": act_kept, "dve_kept": dve_kept}

        N_CONST = 6
        with nc.Block() as block:

            @block.sync
            def _(sp):
                sp.dma_start(w_lr[:, :, :], A["w_lr"]).then_inc(gate_in, 16)
                for dst, src in ((ident, "ident"), (causal, "causal"), (own_rows, "own_rows")):
                    sp.dma_start(dst[:], A[src]).then_inc(const_in, 16)
                sp.dma_start(w[:, :, :], A["w_gla"][0]).then_inc(w_in, 16)
                sp.wait_ge(w_in, 16)
                sp.wait_ge(const_in, 16 * N_CONST)

            @block.scalar
            def _(act):
                for n in range(2):
                    act.dma_start(goes_on[:, n, :], A["goes_on"][n].partition_broadcast(P)).then_inc(const_in, 16)
                act.dma_start(norm_w[:, :], A["gla_norm"][0].partition_broadcast(P)).then_inc(const_in, 16)
                for g in range(CHUNKS):
                    act.wait_ge(lr_full, g + 1)
                    act.activation(lrT[:, g * CHUNK:(g + 1) * CHUNK], banks[g][0:RANK, 0:CHUNK], ACT.Copy).then_inc(act_kept, 1)

            @block.tensor
            def _(pe):
                pe.wait_ge(gate_in, 16)
                for g in range(CHUNKS):
                    for k in range(KC):
                        last = pe.matmul(banks[g][0:RANK, 0:CHUNK], w_lr[:, k, :], hT[:, k, g * CHUNK:(g + 1) * CHUNK], start=(k == 0), stop=(k == KC - 1))
                    last.then_inc(lr_full, 1)

            @block.vector
            def _(dve):
                dve.memset(kl[:, :, :, :], 0.0).then_inc(zeroed, 1)
                dve.memset(q_own[:, :], 0.0).then_inc(zeroed, 1)
        S.rest()

        groups = [("gate", n) for n in range(3)] + [("q", n) for n in range(3)] + [("k", n) for n in range(3)] + [("v", n) for n in range(5)]
        OG_FIRST = 4
        keeper = {"gate": "act_kept", "q": "act_kept", "k": "dve_kept", "v": "dve_kept"}
        count, kept_at = {"act_kept": 0, "dve_kept": 0}, []
        for what, _ in groups:
            count[keeper[what]] += 1
            kept_at.append((keeper[what], count[keeper[what]]))

        def two_tiles(n):
            return 1 if 2 * n + 1 == TILES else 2

        att_bank, kdT_bank, u_bank, o_bank, oT_bank = banks[0:2], banks[2], banks[3], banks[4:6], banks[6:8]
        by_tile = lambda x: x[:, 0:PROMPT].rearrange("p (t n) -> p t n", n=P)
        by_seq = lambda x: x[:, PROMPT:TOK].rearrange("p (s n) -> p s n", n=NEW)

        with nc.Fori(0, GLA_HEADS) as head:
            with nc.Block() as block:

                @block.sync
                def _(sp):
                    sp.dma_start(w_gate[:, :], A["w_gate"][:, bass.ds(head * DK, DK)]).then_inc(gate_in, 16)
                    sp.dma_start(b_gate[:, :], A["b_gate"][head]).then_inc(gate_in, 16)
                    sp.dma_start(s0[:, :, :], A["s0"][head]).then_inc(s0_in, 16)
                    sp.wait_ge(proj_full, len(groups))
                    sp.wait_ge(og_full, TILES)
                    sp.dma_start(w[:, :, :], A["w_gla"][head + 1]).then_inc(w_in, 16)
                    sp.wait_ge(state_ready, PTILES)
                    sp.dma_start(prompt_state[head], state[:, PTILES % 2, :]).then_inc(stored, 16)
                    sp.wait_ge(s0_ready, SEQS)
                    sp.dma_start(sample_state[head], s0[:, :, :]).then_inc(stored, 16)
                    sp.wait_ge(oT_kept, TILES)
                    sp.dma_start(oA_dram[bass.ds(2 * head, 2)].rearrange("k p t -> p k t"), oT[:, :, :]).then_inc(stored, 16)
                    sp.wait_ge(w_in, 16)
                    sp.wait_ge(stored, 48)

                @block.tensor
                def _(pe):
                    pe.wait_ge(gate_in, 32)
                    for g, (what, n) in enumerate(groups):
                        if g >= 8:
                            pe.wait_ge(kept[kept_at[g - 8][0]], kept_at[g - 8][1])
                        bank = banks[g % 8]
                        cols = slice(n * CHUNK, (n + 1) * CHUNK)
                        if what == "gate":
                            last = pe.matmul(bank[:, 0:CHUNK], w_gate[:, :], lrT[:, cols], start=True, stop=True)
                        elif what in "qk":
                            w0 = DK * "qk".index(what)
                            for k in range(KC):
                                last = pe.matmul(bank[:, 0:CHUNK], w[:, k, w0:w0 + DK], hT[:, k, cols], start=(k == 0), stop=(k == KC - 1))
                        else:
                            w0 = 2 * DK
                            for u in range(two_tiles(n)):
                                tile = 2 * n + u
                                for k in range(KC):
                                    last = pe.matmul(bank[:, u * DV:(u + 1) * DV], hT[:, k, tile * P:(tile + 1) * P], w[:, k, w0:w0 + DV],
                                                     start=(k == 0), stop=(k == KC - 1))
                        last.then_inc(proj_full, 1)

                    def output_gate(t):
                        if t < 2:
                            pe.wait_ge(dve_kept, 1 + t)
                        else:
                            pe.wait_ge(og_kept, t - 1)
                        for k in range(KC):
                            last = pe.matmul(oT_bank[t % 2][:, 0:DV], hT[:, k, t * P:(t + 1) * P], w[:, k, 2 * DK + DV:2 * DK + 2 * DV], start=(k == 0), stop=(k == KC - 1))
                        last.then_inc(og_full, 1)

                    for t in range(OG_FIRST):
                        output_gate(t)
                    pe.wait_ge(act_kept, count["act_kept"])
                    pe.wait_ge(dve_kept, count["dve_kept"])
                    pe.wait_ge(products, 3)

                    def scores(n):
                        pe.wait_ge(kl_ready, n + 1)
                        if n >= 2:
                            pe.wait_ge(att_ready, n - 1)
                        for s in range(SUBS):
                            cols = slice(s * SUB, (s + 1) * SUB)
                            last = pe.matmul(att_bank[n % 2][:, cols], kl[:, n % KL, s, :], ec[:, n * P + s * SUB:n * P + (s + 1) * SUB], start=True, stop=True)
                        last.then_inc(att_full, 1)
                        if n >= 1:
                            pe.wait_ge(kdn_ready, n)
                        pe.transpose(kdT_bank[:, 0:P], kd[:, n * P:(n + 1) * P], ident[:, :]).then_inc(kdT_full, 1)

                    def outputs(n):
                        pe.wait_ge(att_ready, n + 1)
                        if n >= 2:
                            pe.wait_ge(o_kept, n - 1)
                        out = o_bank[n % 2][:, 0:DV]
                        last = pe.matmul(out, att[:, n % 2, :], v[:, n, :], start=True, stop=(n == 0))
                        if n:
                            pe.wait_ge(state_ready, n)
                            last = pe.matmul(out, eb[:, n * P:(n + 1) * P], state[:, n % 2, :], start=False, stop=True)
                        last.then_inc(o_full, 1)
                        pe.wait_ge(kdn_ready, n + 1)
                        pe.matmul(u_bank[:, 0:DV], kdn[:, n % 2, :], v[:, n, :], start=True, stop=True).then_inc(u_full, 1)

                    for s in range(1, PTILES + 3):
                        if s - 1 < PTILES:
                            scores(s - 1)
                        if OG_FIRST + s - 1 < TILES:
                            output_gate(OG_FIRST + s - 1)
                        if 0 <= s - 3:
                            outputs(s - 3)

                    n = PTILES
                    pe.wait_ge(kl_ready, n + 1)
                    pe.matmul(att_bank[n % 2][:, 0:P], kl[:, n % KL, 0, :], ec[:, PROMPT:TOK], start=True, stop=True).then_inc(att_full, 1)
                    pe.transpose(kdT_bank[:, 0:P], kd[:, PROMPT:TOK], ident[:, :]).then_inc(kdT_full, 1)
                    pe.wait_ge(att_ready, n + 1)
                    pe.wait_ge(o_kept, n - 1)
                    pe.wait_ge(s0_in, 16)
                    pe.wait_ge(q_split, 1)
                    out = o_bank[n % 2][:, 0:DV]
                    pe.matmul(out, att[:, n % 2, :], v[:, n, :], start=True, stop=False)
                    for s in range(SEQS):
                        last = pe.matmul(out, q_own[:, s * P:(s + 1) * P], s0[:, s, :], start=False, stop=(s == SEQS - 1))
                    last.then_inc(o_full, 1)
                    pe.wait_ge(kdn_ready, n + 1)
                    pe.wait_ge(v_split, SEQS)
                    for s in range(SEQS):
                        if s >= 2:
                            pe.wait_ge(s0_ready, s - 1)
                        else:
                            pe.wait_ge(state_ready, PTILES)
                        pe.matmul((u_bank, kdT_bank)[s % 2][:, 0:DV], kdn[:, n % 2, :], v_own[:, s, :], start=True, stop=True).then_inc(u_full, 1)

                    for t in range(TILES):
                        pe.wait_ge(o_normed, t + 1)
                        if t >= 2:
                            pe.wait_ge(oT_kept, t - 1)
                        for k in range(2):
                            last = pe.transpose(oT_bank[t % 2][:, k * P:(k + 1) * P], o_raw[:, t, k * P:(k + 1) * P], ident[:, :])
                        last.then_inc(oT_full, 1)

                @block.scalar
                def _(act):
                    for g, (what, n) in enumerate(groups):
                        if keeper[what] != "act_kept":
                            continue
                        act.wait_ge(proj_full, g + 1)
                        cols, bank = slice(n * CHUNK, (n + 1) * CHUNK), banks[g % 8]
                        if what == "gate":
                            act.activation(la[:, cols], bank[:, 0:CHUNK], ACT.Identity, bias=b_gate[:, 0:1]).then_inc(act_kept, 1)
                        else:
                            act.activation(qT[:, cols], bank[:, 0:CHUNK], ACT.Copy, scale=DK ** -0.5).then_inc(act_kept, 1)

                    def keep_gate(t):
                        act.wait_ge(og_full, t + 1)
                        act.activation(og[:, t, :], oT_bank[t % 2][:, 0:DV], ACT.Copy).then_inc(og_kept, 1)

                    act.preload_act_table_set("natural_log_exp_and_others")
                    act.wait_ge(capped, 1)
                    act.activation(b[:, :], b[:, :], ACT.Exp, scale=-1.0).then_inc(gate_exp, 1)
                    act.wait_ge(gate_exp, 1)
                    act.activation(b[:, :], b[:, :], ACT.Ln, bias=1.0).then_inc(gate_log, 1)
                    keep_gate(0)
                    keep_gate(1)
                    act.wait_ge(b_ready, 1)
                    act.wait_ge(c_ready, 1)
                    act.activation(ec[:, :], c[:, :], ACT.Exp).then_inc(ec_ready, 1)
                    act.activation(eb[:, :], b[:, :], ACT.Exp).then_inc(eb_ready, 1)
                    act.activation(decay[:, 0:PTILES], by_tile(b)[:, :, P - 1], ACT.Exp).then_inc(decays, 1)
                    act.activation(decay[:, PTILES:], by_seq(b)[:, :, NEW - 1], ACT.Exp).then_inc(decays, 1)
                    keep_gate(2)
                    keep_gate(3)
                    act.wait_ge(kd_diff, 2)
                    act.activation(kd[:, :], kd[:, :], ACT.Exp).then_inc(kd_exp, 1)

                    def key_scales(n):
                        if n >= KL:
                            act.wait_ge(att_full, n - KL + 1)
                        for s in range(SUBS):
                            here = n * P
                            before = b[:, here + s * SUB - 1:here + s * SUB] if s else 0.0
                            last = act.activation(kl[:, n % KL, s, 0:(s + 1) * SUB], b[:, here:here + (s + 1) * SUB], ACT.Exp, bias=before, scale=-1.0)
                        last.then_inc(kl_exp, 1)

                    def rest(n):
                        act.wait_ge(kdT_full, n + 1)
                        if n >= 2:
                            act.wait_ge(u_full, n - 1)
                        act.activation(kdn[:, n % 2, :], kdT_bank[:, 0:P], ACT.Copy).then_inc(kdn_ready, 1)

                    def square(n):
                        act.wait_ge(o_kept, n + 1)
                        if n:
                            act.wait_ge(squared, n)
                        act.activation(junk[:, :], o_raw[:, n, :], ACT.Square, accum_out=squares[:, n:n + 1]).then_inc(squared, 1)

                    for s in range(PTILES + 4):
                        if s < PTILES:
                            key_scales(s)
                        if s == PTILES:
                            act.wait_ge(att_full, s - KL + 1)
                            act.activation(kl[:, s % KL, 0, :], c[:, PROMPT:TOK], ACT.Exp, scale=-1.0).then_inc(kl_exp, 1)
                        if 0 <= s - 2 < PTILES:
                            rest(s - 2)
                        if 0 <= s - 2 and OG_FIRST + s - 2 < TILES:
                            keep_gate(OG_FIRST + s - 2)
                        if 0 <= s - 4:
                            square(s - 4)
                    n = PTILES
                    rest(n)
                    act.wait_ge(og_kept, TILES)
                    act.activation(og[:, :, :], og[:, :, :], ACT.Silu).then_inc(og_silu, 1)
                    square(n)
                    act.wait_ge(mean_inv, 1)
                    act.activation(rms[:, :], rms[:, :], ACT.Sqrt).then_inc(root, 1)
                    for t in range(TILES):
                        act.wait_ge(oT_full, t + 1)
                        act.activation(oT[:, :, t * P:(t + 1) * P], oT_bank[t % 2][:, 0:2 * P].rearrange("p (k n) -> p k n", k=2), ACT.Copy).then_inc(oT_kept, 1)

                @block.vector
                def _(dve):
                    for g, (what, n) in enumerate(groups):
                        if keeper[what] == "dve_kept":
                            dve.wait_ge(proj_full, g + 1)
                            bank = banks[g % 8]
                            if what == "k":
                                dve.tensor_copy(kT[:, n * CHUNK:(n + 1) * CHUNK], bank[:, 0:CHUNK]).then_inc(dve_kept, 1)
                            else:
                                m = two_tiles(n)
                                dve.tensor_copy(v[:, 2 * n:2 * n + m, :].rearrange("p t n -> p (t n)"), bank[:, 0:m * DV]).then_inc(dve_kept, 1)
                        if g == 3:
                            dve.wait_ge(act_kept, 3)
                            dve.tensor_scalar(b[:, :], la[:, :], -20.0, None, ALU.max).then_inc(capped, 1)
                        if g == 8:
                            dve.wait_ge(gate_log, 1)
                            dve.scalar_tensor_tensor(la[:, :], b[:, :], -1.0, la[:, :], ALU.mult, ALU.min).then_inc(la_min, 1)
                            dve.wait_ge(la_min, 1)
                            dve.tensor_scalar(la[:, :], la[:, :], 1.0 / TAU, None, ALU.mult).then_inc(la_ready, 1)
                            dve.wait_ge(la_ready, 1)
                            dve.tensor_tensor_scan(b[:, :], goes_on[:, 0, :], la[:, :], 0.0, ALU.mult, ALU.add).then_inc(b_ready, 1)
                            dve.tensor_tensor_scan(c[:, :], goes_on[:, 1, :], la[:, :], 0.0, ALU.mult, ALU.add).then_inc(c_ready, 1)
                    for s in range(SEQS):
                        if s == 0:
                            dve.wait_ge(dve_kept, count["dve_kept"])
                        dve.tensor_scalar(v_own[:, s, :], v[:, TILES - 1, :], own_rows[:, s:s + 1], None, ALU.mult).then_inc(v_split, 1)
                    dve.wait_ge(b_ready, 1)
                    for x, out in ((by_tile(b), by_tile(kd)), (by_seq(b), by_seq(kd))):
                        last = x[:, :, x.shape[2] - 1:x.shape[2]].broadcast_to(x.shape)
                        dve.tensor_tensor(out, last, x, ALU.subtract).then_inc(kd_diff, 1)
                    dve.wait_ge(act_kept, count["act_kept"])
                    dve.wait_ge(ec_ready, 1)
                    dve.tensor_tensor(ec[:, :], ec[:, :], qT[:, :], ALU.mult).then_inc(products, 1)
                    dve.wait_ge(eb_ready, 1)
                    dve.tensor_tensor(eb[:, :], eb[:, :], qT[:, :], ALU.mult).then_inc(products, 1)
                    dve.wait_ge(kd_exp, 1)
                    dve.tensor_tensor(kd[:, :], kd[:, :], kT[:, :], ALU.mult).then_inc(products, 1)
                    dve.wait_ge(products, 2)
                    dve.tensor_copy(q_own[:, :].rearrange("p (s n) -> p s n", n=P + NEW)[:, :, 0:NEW], by_seq(eb)).then_inc(q_split, 1)

                    def scale_keys(n):
                        dve.wait_ge(kl_exp, n + 1)
                        if n < PTILES:
                            keys = kT[:, n * P:(n + 1) * P].unsqueeze(1).broadcast_to([P, SUBS, P])
                            dve.tensor_tensor(kl[:, n % KL], kl[:, n % KL], keys, ALU.mult).then_inc(kl_ready, 1)
                        else:
                            dve.tensor_tensor(kl[:, n % KL, 0, :], kl[:, n % KL, 0, :], kT[:, PROMPT:TOK], ALU.mult).then_inc(kl_ready, 1)

                    def hide_future(n):
                        dve.wait_ge(att_full, n + 1)
                        if n >= 2:
                            dve.wait_ge(o_full, n - 1)
                        dve.tensor_tensor(att[:, n % 2, :], att_bank[n % 2][:, 0:P], causal[:, n // PTILES, :], ALU.mult).then_inc(att_ready, 1)

                    def next_state(n):
                        dve.wait_ge(u_full, n + 1)
                        if n == 0:
                            dve.tensor_copy(state[:, 1, :], u_bank[:, 0:DV]).then_inc(state_ready, 1)
                        else:
                            dve.wait_ge(state_ready, n)
                            dve.wait_ge(decays, 1)
                            dve.scalar_tensor_tensor(state[:, (n + 1) % 2, :], state[:, n % 2, :], decay[:, n:n + 1], u_bank[:, 0:DV],
                                                     ALU.mult, ALU.add).then_inc(state_ready, 1)

                    def keep_output(n):
                        dve.wait_ge(o_full, n + 1)
                        dve.tensor_copy(o_raw[:, n, :], o_bank[n % 2][:, 0:DV]).then_inc(o_kept, 1)

                    for s in range(PTILES + 4):
                        if 0 <= s - 4:
                            next_state(s - 4)
                            keep_output(s - 4)
                        if 0 <= s - 2 < PTILES:
                            hide_future(s - 2)
                        if s <= PTILES:
                            scale_keys(s)
                    n = PTILES
                    hide_future(n)
                    keep_output(n)
                    for s in range(SEQS):
                        dve.wait_ge(u_full, PTILES + s + 1)
                        dve.wait_ge(decays, 2)
                        dve.scalar_tensor_tensor(s0[:, s, :], s0[:, s, :], decay[:, PTILES + s:PTILES + s + 1], (u_bank, kdT_bank)[s % 2][:, 0:DV],
                                                 ALU.mult, ALU.add).then_inc(s0_ready, 1)
                    dve.wait_ge(og_silu, 1)
                    dve.tensor_tensor(og[:, :, :], og[:, :, :], norm_w[:, :].unsqueeze(1).broadcast_to([P, TILES, DV]), ALU.mult).then_inc(og_scaled, 1)
                    dve.wait_ge(squared, TILES)
                    dve.tensor_scalar(rms[:, :], squares[:, :], 1.0 / DV, RMS_EPS, ALU.mult, ALU.add).then_inc(mean_sq, 1)
                    dve.wait_ge(mean_sq, 1)
                    dve.reciprocal(rms[:, :], rms[:, :]).then_inc(mean_inv, 1)
                    dve.wait_ge(root, 1)
                    dve.wait_ge(og_scaled, 1)
                    dve.wait_ge(o_kept, TILES)
                    for t in range(TILES):
                        dve.scalar_tensor_tensor(o_raw[:, t, :], o_raw[:, t, :], rms[:, t:t + 1], og[:, t, :], ALU.mult, ALU.mult).then_inc(o_normed, 1)
            S.rest()


def mix_phase(nc, A, hT, oA_dram, oB_dram, mixT_dram):
    U = 4
    with ExitStack() as ctx:
        S = Scope(nc, ctx, "mix")
        oA, oB = S.sb("oA", [P, KC, TOK]), S.sb("oB", [P, KC, TOK])
        w = S.sb("w", [P, 2, 4, KC, P])
        sg = S.sb("sg", [P, 2, 2, CHUNK])
        part = S.sb("part", [P, 2, 2, CHUNK])
        mixed = S.sb("mixed", [P, 2, TOK])
        banks = [S.ps(f"bank{i}", [P, HALF]) for i in range(8)]
        o_in, next_in = S.sem("o_in"), S.sem("next_in")
        w_in = [S.sem(f"w_in{n}") for n in range(2)]
        full, gated, parts, mixed_ready, stored = S.sem("full"), S.sem("gated"), S.sem("parts"), S.sem("mixed_ready"), [S.sem(f"stored{n}") for n in range(2)]
        with nc.Block() as block:

            @block.sync
            def _(sp):
                sp.dma_start(w[:, 0], A["w_mix"][0]).then_inc(next_in, 16)
                sp.dma_start(oA[:, :, :], oA_dram.rearrange("k p t -> p k t")).then_inc(o_in, 16)
                sp.dma_start(oB[:, :, :], oB_dram.rearrange("k p t -> p k t")).then_inc(o_in, 16)
                sp.wait_ge(next_in, 16)
                sp.wait_ge(o_in, 32)
        S.rest()
        with nc.Fori(0, KC // U) as turn:
            with nc.Block() as block:

                @block.sync
                def _(sp):
                    sp.dma_start(w[:, 1], A["w_mix"][U * turn + 1]).then_inc(w_in[1], 16)
                    for u in range(1, U):
                        sp.wait_ge(full, 4 * CHUNKS * u)
                        if u + 1 < U:
                            sp.dma_start(w[:, (u + 1) % 2], A["w_mix"][U * turn + u + 1]).then_inc(w_in[(u + 1) % 2], 16)
                        else:
                            sp.dma_start(w[:, 0], A["w_mix"][U * turn + U]).then_inc(next_in, 16)
                        sp.wait_ge(mixed_ready, CHUNKS * u)
                        sp.dma_start(mixT_dram[U * turn + u - 1], mixed[:, (u - 1) % 2, :]).then_inc(stored[(u - 1) % 2], 16)
                    sp.wait_ge(mixed_ready, CHUNKS * U)
                    sp.dma_start(mixT_dram[U * turn + U - 1], mixed[:, (U - 1) % 2, :]).then_inc(stored[(U - 1) % 2], 16)
                    sp.wait_ge(next_in, 16)
                    for n in range(2):
                        sp.wait_ge(stored[n], 16 * (U // 2))

                @block.tensor
                def _(pe):
                    for n in range(U * CHUNKS):
                        u, c = n // CHUNKS, n % CHUNKS
                        if c == 0 and u:
                            pe.wait_ge(w_in[u % 2], 16 * ((u + 1) // 2))
                        if n >= 2:
                            pe.wait_ge(gated, 2 * (n - 1))
                            pe.wait_ge(parts, 2 * (n - 1))
                        for m, x in enumerate((hT, hT, oA, oB)):
                            for k in range(KC):
                                last = pe.matmul(banks[4 * (n % 2) + m][:, 0:CHUNK], w[:, u % 2, m, k, :], x[:, k, c * CHUNK:(c + 1) * CHUNK],
                                                 start=(k == 0), stop=(k == KC - 1))
                            last.then_inc(full, 1)

                @block.scalar
                def _(act):
                    for n in range(U * CHUNKS):
                        for m in range(2):
                            act.wait_ge(full, 4 * n + m + 1)
                            if n >= 2:
                                act.wait_ge(parts, 2 * (n - 2) + m + 1)
                            act.activation(sg[:, n % 2, m, :], banks[4 * (n % 2) + m][:, 0:CHUNK], ACT.Sigmoid).then_inc(gated, 1)

                @block.vector
                def _(dve):
                    for n in range(U * CHUNKS):
                        u, c = n // CHUNKS, n % CHUNKS
                        for m in range(2):
                            dve.wait_ge(full, 4 * n + m + 3)
                            dve.wait_ge(gated, 2 * n + m + 1)
                            if n >= 2:
                                dve.wait_ge(mixed_ready, n - 1)
                            dve.tensor_tensor(part[:, n % 2, m, :], sg[:, n % 2, m, :], banks[4 * (n % 2) + 2 + m][:, 0:CHUNK], ALU.mult).then_inc(parts, 1)
                        dve.wait_ge(parts, 2 * n + 2)
                        if c == 0 and u >= 2:
                            dve.wait_ge(stored[u % 2], 16 * (u // 2))
                        dve.tensor_tensor(mixed[:, u % 2, c * CHUNK:(c + 1) * CHUNK], part[:, n % 2, 0, :], part[:, n % 2, 1, :], ALU.add).then_inc(mixed_ready, 1)
            S.rest()


def residual_phase(nc, A, modb, mixT_dram, x1_dram, h2_dram, h2T_dram):
    U = 3
    MW = 3 * D
    with ExitStack() as ctx:
        S = Scope(nc, ctx, "res")
        ident, w_o = S.sb("ident", [P, P]), S.sb("w_o", [P, KC, D])
        ln1 = S.sb("ln1", [P, 2 * D])
        mods = S.sb("mods", [P, 2, MW])
        mT = S.sb("mT", [P, U, KC, P])
        x, x1, h2 = S.sb("x", [P, U, D]), S.sb("x1", [P, U, D]), S.sb("h2", [P, U, D])
        h2T = S.sb("h2T", [P, U, KC, P])
        stats, mv, rstd = S.sb("stats", [P, 2 * U, 2, 6]), S.sb("mv", [P, 2 * U, 2]), S.sb("rstd", [P, 2 * U])
        y = [[S.ps(f"y{i}{c}", [P, HALF]) for c in range(2)] for i in range(2)]
        turned = [S.ps(f"turned{i}", [P, 4, P]) for i in range(2)]
        const_in, mods_in = S.sem("const_in"), S.sem("mods_in")
        m_in, x_in = [S.sem(f"m_in{u}") for u in range(U)], [S.sem(f"x_in{u}") for u in range(U)]
        y_full, y_used, summed, normed, inverse, x1_steps, h2_steps = (S.sem(n) for n in ("y_full", "y_used", "summed", "normed", "inverse", "x1_steps", "h2_steps"))
        turned_full, h2T_kept, stored = S.sem("turned_full"), S.sem("h2T_kept"), S.sem("stored")
        tiles = lambda a: a.rearrange("(t p) n -> t p n", p=P)
        with nc.Block() as block:

            @block.sync
            def _(sp):
                sp.dma_start(w_o[:, :, :], A["w_o"]).then_inc(const_in, 16)
                sp.dma_start(ident[:, :], A["ident"]).then_inc(const_in, 16)
                sp.dma_start(mods[:, 0, :], modb[0, :, 2 * D:5 * D]).then_inc(const_in, 16)
                sp.dma_start(ln1[:, :], A["ln1"][0].partition_broadcast(P)).then_inc(const_in, 16)
                sp.wait_ge(const_in, 64)
        S.rest()
        with nc.Fori(0, TILES // U) as i:
            with nc.Block() as block:

                @block.sync
                def _(sp):
                    for u in range(U):
                        sp.dma_start(mT[:, u], mixT_dram.rearrange("k p t -> p k t")[:, :, bass.ds(U * P * i + P * u, P)]).then_inc(m_in[u], 16)
                        sp.dma_start(x[:, u, :], tiles(A["x"])[U * i + u]).then_inc(x_in[u], 16)
                    sp.dma_start(mods[:, 1, :], modb[i // 2, :, 2 * D:5 * D]).then_inc(mods_in, 16)
                    for u in range(U):
                        sp.wait_ge(x1_steps, 2 * u + 2)
                        sp.dma_start(tiles(x1_dram)[U * i + u], x1[:, u, :]).then_inc(stored, 16)
                        sp.wait_ge(h2_steps, 2 * u + 2)
                        sp.dma_start(tiles(h2_dram)[U * i + u], h2[:, u, :]).then_inc(stored, 16)
                        sp.wait_ge(h2T_kept, 2 * u + 2)
                        sp.dma_start(h2T_dram[U * i + u], h2T[:, u].rearrange("p k n -> p (k n)")).then_inc(stored, 16)
                    sp.wait_ge(stored, 16 * 3 * U)

                @block.tensor
                def _(pe):
                    def turn(u):
                        pe.wait_ge(h2_steps, 2 * u + 2)
                        for c in range(2):
                            n = 2 * u + c
                            if n >= 2:
                                pe.wait_ge(h2T_kept, n - 1)
                            for k in range(4):
                                last = pe.transpose(turned[c][:, k, :], h2[:, u, (4 * c + k) * P:(4 * c + k + 1) * P], ident[:, :])
                            last.then_inc(turned_full, 1)

                    for u in range(U):
                        pe.wait_ge(m_in[u], 16)
                        if u >= 2:
                            pe.wait_ge(y_used, 2 * (u - 1))
                        for c in range(2):
                            for k in range(KC):
                                last = pe.matmul(y[u % 2][c][:, :], mT[:, u, k, :], w_o[:, k, c * HALF:(c + 1) * HALF], start=(k == 0), stop=(k == KC - 1))
                            last.then_inc(y_full, 1)
                        if u:
                            turn(u - 1)
                    turn(U - 1)

                @block.scalar
                def _(act):
                    def root(n):
                        act.wait_ge(normed, 6 * n + 5)
                        act.activation(rstd[:, n:n + 1], rstd[:, n:n + 1], ACT.Sqrt).then_inc(inverse, 1)

                    for u in range(U):
                        root(2 * u)
                        root(2 * u + 1)
                        for c in range(2):
                            act.wait_ge(turned_full, 2 * u + c + 1)
                            act.activation(h2T[:, u, 4 * c:4 * c + 4, :], turned[c][:, :, :], ACT.Copy).then_inc(h2T_kept, 1)

                @block.vector
                def _(dve):
                    n = 0
                    for u in range(U):
                        m = mods[:, u // 2, :]
                        if u == 2:
                            dve.wait_ge(mods_in, 16)
                        for c in range(2):
                            dve.wait_ge(y_full, 2 * u + c + 1)
                            dve.tensor_tensor(x1[:, u, c * HALF:(c + 1) * HALF], y[u % 2][c][:, :], m[:, c * HALF:(c + 1) * HALF], ALU.mult).then_inc(y_used, 1)
                        dve.wait_ge(x_in[u], 16)
                        dve.wait_ge(y_used, 2 * u + 2)
                        dve.scalar_tensor_tensor(x[:, u, :], x[:, u, :], ALPHA, x1[:, u, :], ALU.mult, ALU.add).then_inc(summed, 1)
                        dve.wait_ge(summed, u + 1)
                        n = layer_norm_steps(dve, normed, inverse, 2 * u, n, x[:, u, :], stats[:, 2 * u], mv[:, 2 * u], rstd[:, 2 * u:2 * u + 1], x[:, u, :])
                        dve.wait_ge(normed, n)
                        dve.tensor_tensor(x1[:, u, :], x[:, u, :], ln1[:, 0:D], ALU.mult).then_inc(x1_steps, 1)
                        dve.wait_ge(x1_steps, 2 * u + 1)
                        dve.tensor_tensor(x1[:, u, :], x1[:, u, :], ln1[:, D:2 * D], ALU.add).then_inc(x1_steps, 1)
                        dve.wait_ge(x1_steps, 2 * u + 2)
                        n = layer_norm_steps(dve, normed, inverse, 2 * u + 1, n, x1[:, u, :], stats[:, 2 * u + 1], mv[:, 2 * u + 1], rstd[:, 2 * u + 1:2 * u + 2], h2[:, u, :])
                        dve.wait_ge(normed, n)
                        dve.scalar_tensor_tensor(h2[:, u, :], m[:, 2 * D:3 * D], 1.0, h2[:, u, :], ALU.add, ALU.mult).then_inc(h2_steps, 1)
                        dve.wait_ge(h2_steps, 2 * u + 1)
                        dve.tensor_tensor(h2[:, u, :], h2[:, u, :], m[:, D:2 * D], ALU.add).then_inc(h2_steps, 1)
            S.rest()


def peer_phase(nc, A, modb, x1_dram, h2_dram, h2T_dram, y_out):
    SLOTS = PEER_HEADS * TOPK
    U = 3
    R = 8
    G = 1
    DG = 8
    with ExitStack() as ctx:
        S = Scope(nc, ctx, "peer")
        ident = S.sb("ident", [P, P])
        w_q, keysT = S.sb("w_q", [P, KC, 2 * PEER_HEADS * P]), S.sb("keysT", [P, 2 * PEER_HEADS, NKEYS])
        ln2 = S.sb("ln2", [P, 2 * D])
        sixteen = S.sb("sixteen", [P, TOPK])
        ring = S.sb("ring", [P, R, 2 * D])
        h2, x1, g2 = S.sb("h2", [P, U, D]), S.sb("x1", [P, 2, D]), S.sb("g2", [P, 2, D])
        h2T = S.sb("h2T", [P, U, KC, P])
        diag = S.sb("diag", [P, DG, P])
        dots, act_v, w = S.sb("dots", [P, SLOTS]), S.sb("act_v", [P, SLOTS]), S.sb("w", [P, SLOTS])
        experts, gates = S.sb("experts", [P, U, SLOTS], U32), S.sb("gates", [P, U, SLOTS])
        qs = S.sb("qs", [P, 2, 2, P])
        sc, sc2 = S.sb("sc", [P, 2, 2, NKEYS]), S.sb("sc2", [P, 2, NKEYS])
        top, at = S.sb("top", [P, 2, TOPK]), S.sb("at", [P, 2, TOPK], U32)
        at_f = S.sb("at_f", [P, 2, TOPK])
        cand, cand2 = S.sb("cand", [P, TOPK, TOPK]), S.sb("cand2", [P, TOPK * TOPK])
        best, pos = S.sb("best", [P, TOPK]), S.sb("pos", [P, TOPK], U32)
        part, part_f = S.sb("part", [P, 2, TOPK], U32), S.sb("part_f", [P, 2, TOPK])
        hit = S.sb("hit", [P, 2, TOPK, TOPK])
        ids = S.sb("ids", [P, 2, TOPK])
        shifted, e_sum, e_inv = S.sb("shifted", [P, TOPK]), S.sb("e_sum", [P, 1]), S.sb("e_inv", [P, 1])
        stats, mv, rstd = S.sb("stats", [P, 2, 6]), S.sb("mv", [P, 2]), S.sb("rstd", [P, 1])
        f = [[S.ps(f"f{b}{c}", [P, HALF]) for c in range(2)] for b in range(2)]
        q_bank = [S.ps(f"q{i}", [P, 2, P]) for i in range(2)]
        s_bank = [S.ps(f"s{i}", [P, 2, NKEYS]) for i in range(2)]

        const_in, gate2_in, next_in = S.sem("const_in"), S.sem("gate2_in"), S.sem("next_in")
        h2T_in, h2_in, x1_in = ([S.sem(f"{n}{u}") for u in range(U)] for n in ("h2T_in", "h2_in", "x1_in"))
        w_q_in = [S.sem(f"w_q_in{n}") for n in range(2)]
        ring_in = [S.sem(f"ring_in{r}") for r in range(R)]
        dot_done, gelu_done, w_ready, diag_ready, v_used = (S.sem(n) for n in ("dot_done", "gelu_done", "w_ready", "diag_ready", "v_used"))
        q_full, q_kept, s_full, s_kept = (S.sem(n) for n in ("q_full", "q_kept", "s_full", "s_kept"))
        chosen, exp_done = S.sem("chosen"), S.sem("exp_done")
        f_read, normed, inverse, ended, stored = S.sem("f_read"), S.sem("normed"), S.sem("inverse"), S.sem("ended"), S.sem("stored")

        GROUPS = SLOTS // G
        END = 4 // G - 1
        KEYS_AT, PARTS_AT, EXP_AT = 4, 8, 12

        def query_matmuls(pe, h, tile):
            head = h % PEER_HEADS
            if h >= 2:
                pe.wait_ge(q_kept, h - 1)
            for p in range(2):
                for k in range(KC):
                    last = pe.matmul(q_bank[h % 2][:, p, :], w_q[:, k, (2 * head + p) * P:(2 * head + p + 1) * P], h2T[:, tile, k, :], start=(k == 0), stop=(k == KC - 1))
            last.then_inc(q_full, 1)

        def key_matmuls(pe, h):
            pe.wait_ge(q_kept, h + 1)
            if h >= 2:
                pe.wait_ge(s_kept, h - 1)
            for p in range(2):
                last = pe.matmul(s_bank[h % 2][:, p, :], qs[:, h % 2, p, :], keysT[:, 2 * (h % PEER_HEADS) + p, :], start=True, stop=True)
            last.then_inc(s_full, 1)

        def keep_query(act, h):
            act.wait_ge(q_full, h + 1)
            if h >= 2:
                act.wait_ge(s_full, h - 1)
            act.activation(qs[:, h % 2], q_bank[h % 2][:, :, :], ACT.Copy).then_inc(q_kept, 1)

        def keep_scores(act, h):
            act.wait_ge(s_full, h + 1)
            if h >= 2:
                act.wait_ge(chosen, CHOOSE * (h - 1))
            act.activation(sc[:, h % 2], s_bank[h % 2][:, :, :], ACT.Copy).then_inc(s_kept, 1)

        def exp_best(act, h):
            act.wait_ge(chosen, CHOOSE * h + SHIFTED)
            act.activation(shifted[:, :], shifted[:, :], ACT.Exp, accum_out=e_sum[:, 0:1]).then_inc(exp_done, 1)

        CHOOSE, PARTS, SHIFTED = 27, 11, 18

        def counting(dve, step):
            def did(ins):
                ins.then_inc(chosen, 1)
                step[0] += 1

            def so_far(back=0):
                dve.wait_ge(chosen, step[0] - back)

            return did, so_far

        def choose_parts(dve, h):

            step = [CHOOSE * h]
            did, so_far = counting(dve, step)
            s = sc[:, h % 2]
            dve.wait_ge(s_kept, h + 1)
            so_far()
            for p in range(2):
                did(dve.max(top[:, p, 0:8], s[:, p, :]))
            for p in range(2):
                so_far(1)
                did(dve.max_index(at[:, p, 0:8], top[:, p, 0:8], s[:, p, :]))
                did(dve.match_replace(sc2[:, p, :], top[:, p, 0:8], s[:, p, :], NEG))
            so_far()
            for p in range(2):
                did(dve.max(top[:, p, 8:16], sc2[:, p, :]))
            so_far()
            for p in range(2):
                did(dve.max_index(at[:, p, 8:16], top[:, p, 8:16], sc2[:, p, :]))
            did(dve.tensor_tensor(cand[:, :, :], top[:, 0, :].unsqueeze(2).broadcast_to([P, TOPK, TOPK]),
                                  top[:, 1, :].unsqueeze(1).broadcast_to([P, TOPK, TOPK]), ALU.add))
            assert step[0] == CHOOSE * h + PARTS

        def choose_best(dve, h, tile):
            step = [CHOOSE * h + PARTS]
            did, so_far = counting(dve, step)
            so_far()
            flat = cand[:, :, :].rearrange("p i j -> p (i j)")
            did(dve.max(best[:, 0:8], flat))
            did(dve.tensor_copy(at_f[:, :, :], at[:, :, :]))
            so_far()
            did(dve.match_replace(cand2[:, :], best[:, 0:8], flat, NEG))
            did(dve.max_index(pos[:, 0:8], best[:, 0:8], flat))
            so_far()
            did(dve.max(best[:, 8:16], cand2[:, :]))
            so_far()
            did(dve.max_index(pos[:, 8:16], best[:, 8:16], cand2[:, :]))
            did(dve.tensor_scalar(shifted[:, :], best[:, :], best[:, 0:1], None, ALU.subtract))
            assert step[0] == CHOOSE * h + SHIFTED
            so_far(1)
            did(dve.tensor_single_scalar(part[:, 0, :], pos[:, :], 4, ALU.logical_shift_right))
            did(dve.tensor_single_scalar(part[:, 1, :], pos[:, :], TOPK - 1, ALU.bitwise_and))
            so_far()
            did(dve.tensor_copy(part_f[:, :, :], part[:, :, :]))
            so_far()
            did(dve.tensor_tensor(hit[:, :, :, :].rearrange("p a i j -> p (a i) j"), part_f[:, :, :].rearrange("p a i -> p (a i)").unsqueeze(2).broadcast_to([P, 2 * TOPK, TOPK]),
                                  sixteen[:, :].unsqueeze(1).broadcast_to([P, 2 * TOPK, TOPK]), ALU.is_equal))
            so_far()
            did(dve.tensor_tensor(hit[:, :, :, :], hit[:, :, :, :], at_f[:, :, :].unsqueeze(2).broadcast_to([P, 2, TOPK, TOPK]), ALU.mult))
            so_far()
            did(dve.tensor_reduce(ids[:, :, :].rearrange("p a i -> p (a i)"), hit[:, :, :, :].rearrange("p a i j -> p (a i) j"), AX_X, ALU.add))
            dve.wait_ge(exp_done, h + 1)
            did(dve.reciprocal(e_inv[:, :], e_sum[:, :]))
            so_far()
            cols = slice(h % PEER_HEADS * TOPK, (h % PEER_HEADS + 1) * TOPK)
            did(dve.scalar_tensor_tensor(experts[:, tile, cols], ids[:, 0, :], float(NKEYS), ids[:, 1, :], ALU.mult, ALU.add))
            did(dve.tensor_scalar(gates[:, tile, cols], shifted[:, :], e_inv[:, 0:1], None, ALU.mult))
            assert step[0] == CHOOSE * (h + 1)

        def fetch(pool, slot, tile, k):
            pool.indirect_dma_start(ring[:, slot % R, :], None, A["uv"], bass.IndirectOffsetOnAxis(ap=experts[:, tile, k:k + 1], axis=0)).then_inc(ring_in[slot % R], 16)

        def rest_fetches(pool, each):
            for r in range(R):
                pool.wait_ge(ring_in[r], 16 * each)
            pool.dma_reset(range(ring_in[0].num, ring_in[-1].num + 1))

        rows = lambda a: a.rearrange("(t p) n -> t p n", p=P)
        flat_h2T = lambda u: h2T[:, u].rearrange("p k n -> p (k n)")
        with nc.Block() as block:

            @block.sync
            def _(sp):
                sp.dma_start(flat_h2T(0), h2T_dram[0]).then_inc(h2T_in[0], 16)
                for n, cols in enumerate((slice(0, 2 * P), slice(2 * P, 2 * PEER_HEADS * P))):
                    sp.dma_start(w_q[:, :, cols], A["w_q"][:, :, cols]).then_inc(w_q_in[n], 16)
                    if n == 0:
                        sp.dma_start(keysT[:, :, :], A["keysT"]).then_inc(const_in, 16)
                        sp.dma_start(sixteen[:, :], A["sixteen"]).then_inc(const_in, 16)
                sp.dma_start(ident[:, :], A["ident"]).then_inc(next_in, 16)
                sp.dma_start(ln2[:, :], A["ln2"][0].partition_broadcast(P)).then_inc(next_in, 16)
                sp.dma_start(flat_h2T(1), h2T_dram[1]).then_inc(next_in, 16)
                sp.dma_start(h2[:, 0, :], rows(h2_dram)[0]).then_inc(next_in, 16)
                sp.dma_start(g2[:, 0, :], modb[0, :, 5 * D:6 * D]).then_inc(next_in, 16)
                sp.wait_ge(next_in, 80)

            @block.gpsimd
            def _(pool):
                pool.wait_ge(chosen, CHOOSE)
                for r in range(R):
                    fetch(pool, r, 0, r)
                rest_fetches(pool, 1)

            @block.tensor
            def _(pe):
                pe.wait_ge(h2T_in[0], 16)
                for h in range(PEER_HEADS):
                    if h < 2:
                        pe.wait_ge(w_q_in[h], 16)
                    query_matmuls(pe, h, 0)
                    if h == 1:
                        pe.wait_ge(const_in, 32)
                    if h:
                        key_matmuls(pe, h - 1)
                key_matmuls(pe, PEER_HEADS - 1)

            @block.scalar
            def _(act):
                for h in range(PEER_HEADS):
                    keep_query(act, h)
                    keep_scores(act, h)
                    exp_best(act, h)

            @block.vector
            def _(dve):
                dve.wait_ge(const_in, 32)
                for h in range(PEER_HEADS):
                    choose_parts(dve, h)
                    choose_best(dve, h, 0)
        S.rest()

        with nc.Fori(0, TILES // U) as i:
            with nc.Block() as block:

                @block.sync
                def _(sp):
                    sp.dma_start(flat_h2T(2), h2T_dram[U * i + 2]).then_inc(h2T_in[2], 16)
                    sp.dma_start(h2[:, 1, :], rows(h2_dram)[U * i + 1]).then_inc(h2_in[1], 16)
                    sp.dma_start(g2[:, 1, :], modb[i // 2, :, 5 * D:6 * D]).then_inc(gate2_in, 16)
                    sp.dma_start(x1[:, 0, :], rows(x1_dram)[U * i]).then_inc(x1_in[0], 16)
                    sp.dma_start(x1[:, 1, :], rows(x1_dram)[U * i + 1]).then_inc(x1_in[1], 16)
                    sp.dma_start(flat_h2T(0), h2T_dram[(U * i + U) % TILES]).then_inc(h2T_in[0], 16)
                    sp.dma_start(h2[:, 2, :], rows(h2_dram)[U * i + 2]).then_inc(h2_in[2], 16)
                    sp.wait_ge(q_full, PEER_HEADS)
                    sp.dma_start(flat_h2T(1), h2T_dram[(U * i + U + 1) % TILES]).then_inc(next_in, 16)
                    for u in range(U):
                        sp.wait_ge(ended, 3 * u + 3)
                        sp.dma_start(rows(y_out)[U * i + u], x1[:, u % 2, :]).then_inc(stored, 16)
                        if u == 0:
                            sp.dma_start(h2[:, 0, :], rows(h2_dram)[(U * i + U) % TILES]).then_inc(next_in, 16)
                            sp.wait_ge(stored, 16)
                            sp.dma_start(x1[:, 0, :], rows(x1_dram)[U * i + 2]).then_inc(x1_in[2], 16)
                    sp.wait_ge(next_in, 32)
                    sp.wait_ge(stored, 48)

                @block.gpsimd
                def _(pool):
                    for n in range(R, U * SLOTS):
                        if n % SLOTS == 0:
                            pool.wait_ge(chosen, CHOOSE * PEER_HEADS * (n // SLOTS))
                        pool.wait_ge(v_used, n - R + 1)
                        fetch(pool, n, n // SLOTS, n % SLOTS)
                    pool.wait_ge(chosen, CHOOSE * PEER_HEADS * U)
                    for r in range(R):
                        pool.wait_ge(v_used, U * SLOTS - R + r + 1)
                        fetch(pool, r, 0, r)
                    rest_fetches(pool, U * SLOTS // R)

                @block.tensor
                def _(pe):
                    for n in range(U * SLOTS):
                        u, k, h = n // SLOTS, n % SLOTS, n // TOPK
                        if n % TOPK == 0:
                            if k == 0 and u:
                                pe.wait_ge(h2T_in[(u + 1) % U], 16)
                            query_matmuls(pe, h, (u + 1) % U)
                        if n % TOPK == KEYS_AT:
                            key_matmuls(pe, h)
                        if k == 0 and u == 2:
                            pe.wait_ge(f_read, 2)
                        pe.wait_ge(diag_ready, n + 1)
                        for c in range(2):
                            last = pe.matmul(f[u % 2][c][:, :], diag[:, n % DG, :], ring[:, n % R, D + c * HALF:D + (c + 1) * HALF], start=(k == 0), stop=(k == SLOTS - 1))
                        last.then_inc(v_used, 1)

                @block.scalar
                def _(act):
                    def root(u):
                        act.wait_ge(normed, 6 * u + 5)
                        act.activation(rstd[:, :], rstd[:, :], ACT.Sqrt).then_inc(inverse, 1)

                    for j in range(U * GROUPS):
                        h, part = j * G // TOPK, j * G % TOPK
                        cols = slice(j % GROUPS * G, (j % GROUPS + 1) * G)
                        act.wait_ge(dot_done, (j + 1) * G)
                        act.activation(act_v[:, cols], dots[:, cols], ACT.Gelu_apprx_tanh).then_inc(gelu_done, 1)
                        if part == EXP_AT:
                            exp_best(act, h)
                        if j % GROUPS == END and j > GROUPS:
                            root(j // GROUPS - 1)
                        act.wait_ge(w_ready, j + 1)
                        for n in range(j * G, (j + 1) * G):
                            if n >= DG:
                                act.wait_ge(v_used, n - DG + 1)
                            act.activation(diag[:, n % DG, :], ident[:, :], ACT.Copy, scale=w[:, n % SLOTS:n % SLOTS + 1]).then_inc(diag_ready, 1)
                        if part == 0:
                            keep_query(act, h)
                        if part == KEYS_AT:
                            keep_scores(act, h)
                    root(U - 1)

                @block.vector
                def _(dve):
                    def weights(j):
                        cols = slice(j % GROUPS * G, (j % GROUPS + 1) * G)
                        dve.wait_ge(gelu_done, j + 1)
                        dve.tensor_tensor(w[:, cols], act_v[:, cols], gates[:, j // GROUPS, cols], ALU.mult).then_inc(w_ready, 1)

                    def end(u):
                        x, g, y = x1[:, u % 2, :], g2[:, u // 2, :], h2[:, u, :]
                        dve.wait_ge(v_used, SLOTS * (u + 1))
                        dve.wait_ge(dot_done, SLOTS * (u + 1))
                        if u == 2:
                            dve.wait_ge(gate2_in, 16)
                        for c in range(2):
                            cols = slice(c * HALF, (c + 1) * HALF)
                            dve.tensor_tensor(y[:, cols], f[u % 2][c][:, :], g[:, cols], ALU.mult).then_inc(f_read, 1)
                        dve.wait_ge(f_read, 2 * u + 2)
                        dve.wait_ge(x1_in[u], 16)
                        dve.scalar_tensor_tensor(x, x, ALPHA, y, ALU.mult, ALU.add).then_inc(ended, 1)
                        dve.wait_ge(ended, 3 * u + 1)
                        n = layer_norm_steps(dve, normed, inverse, u, 6 * u, x, stats[:, :, :], mv[:, :], rstd[:, :], x)
                        dve.wait_ge(normed, n)
                        dve.tensor_tensor(x, x, ln2[:, 0:D], ALU.mult).then_inc(ended, 1)
                        dve.wait_ge(ended, 3 * u + 2)
                        dve.tensor_tensor(x, x, ln2[:, D:2 * D], ALU.add).then_inc(ended, 1)

                    for j in range(U * GROUPS):
                        u, h, part = j // GROUPS, j * G // TOPK, j * G % TOPK
                        if u and j % GROUPS == 0:
                            dve.wait_ge(h2_in[u], 16)
                        for n in range(j * G, (j + 1) * G):
                            v = ring[:, n % R, 0:D]
                            if n >= R:
                                dve.wait_ge(ring_in[n % R], 16 * (n // R))
                            dve.scalar_tensor_tensor(v, v, 1.0, h2[:, u, :], ALU.mult, ALU.mult, accum_out=dots[:, n % SLOTS:n % SLOTS + 1]).then_inc(dot_done, 1)
                            if n % G == (G > 1) and j:
                                weights(j - 1)
                        if part == PARTS_AT:
                            choose_parts(dve, h)
                        if part == EXP_AT:
                            choose_best(dve, h, (u + 1) % U)
                        if j % GROUPS == END and u:
                            end(u - 1)
                    weights(U * GROUPS - 1)
                    end(U - 1)
            S.rest()


def laid_out(i):
    import numpy as np

    f = {k: np.asarray(v) for k, v in i.items()}
    one = {k: f[k][0] for k in ("w_ada", "b_ada", "w_in", "w_gla_gate", "b_gla_gate", "gla_norm_w", "w_gla_proj", "w_sb_proj", "w_o",
                                "ln1_w", "ln1_b", "peer_wq", "peer_keys", "peer_u", "peer_v", "ln2_w", "ln2_b")}

    def rows(w):
        return w.reshape(KC, P, -1).transpose(1, 0, 2)

    cols = np.cumsum([0, 512, 512, 1024, RANK, 1024, 1024, 1024, 1024, 1024, 1024])
    gq, gk, gv, glr, gog, sq, sk, sv, ma, mb = (one["w_in"][:, cols[n]:cols[n + 1]] for n in range(10))

    def padded(blocks):
        return np.concatenate([blocks, blocks[:1]])

    w_sb = padded(np.stack([np.stack([rows(m[:, p * P:(p + 1) * P]) for m in (sq, sk, sv)], 1) for p in range(SB_PAIRS)]))
    w_gla = padded(np.stack([np.concatenate([rows(gq[:, h * DK:(h + 1) * DK]), rows(gk[:, h * DK:(h + 1) * DK]),
                                             rows(gv[:, h * DV:(h + 1) * DV]), rows(gog[:, h * DV:(h + 1) * DV])], 2) for h in range(GLA_HEADS)]))
    w_mix = padded(np.stack([np.stack([rows(m[:, j * P:(j + 1) * P]) for m in (ma, mb, one["w_gla_proj"], one["w_sb_proj"])], 1) for j in range(KC)]))
    cache_k = f["cache_sb_k"][0].reshape(SEQS, PAST, SB_PAIRS, P)
    cache_v = f["cache_sb_v"][0].reshape(SEQS, PBLK, P, SB_PAIRS, P)

    at = np.arange(P)
    s_of, t_of = at // NEW, at % NEW
    q_s, q_t = np.repeat(np.arange(SEQS), 2 * NEW), np.tile(np.arange(NEW), 2 * SEQS)
    hide = np.float32(-1e30)
    tok = np.arange(TOK)
    goes_on = np.stack([np.where(tok < PROMPT, tok % P != 0, tok % NEW != 0), tok % SUB != 0]).astype(np.float32)
    sel = np.zeros((1 + SEQS, 2, P), np.float32)
    sel[0, 0, :] = 1
    sel[1 + s_of, 1, at] = 1
    return {
        "x": np.concatenate([f["x_prompt"].reshape(PROMPT, D), f["x_sample"].reshape(SEQS * NEW, D)]),
        "cT": np.concatenate([f["c_prompt"], f["c_sample"]]).T.reshape(KC, P, 1 + SEQS).transpose(1, 0, 2).reshape(P, -1),
        "w_ada": one["w_ada"], "b_ada": one["b_ada"][None],
        "w_sb": w_sb, "w_gla": w_gla, "w_mix": w_mix, "w_lr": rows(glr),
        "w_gate": one["w_gla_gate"], "b_gate": one["b_gla_gate"].reshape(GLA_HEADS, DK, 1),
        "gla_norm": one["gla_norm_w"][None],
        "w_o": rows(one["w_o"]), "w_q": rows(one["peer_wq"]),
        "keysT": one["peer_keys"].transpose(3, 0, 1, 2).reshape(P, PEER_HEADS * 2, NKEYS),
        "ln1": np.stack([one["ln1_w"], one["ln1_b"]]).reshape(1, 2 * D), "ln2": np.stack([one["ln2_w"], one["ln2_b"]]).reshape(1, 2 * D),
        "uv": np.concatenate([one["peer_u"], one["peer_v"]], 1),
        "kcT": cache_k.transpose(2, 3, 0, 1), "vc": cache_v.transpose(3, 2, 0, 1, 4),
        "s0": f["state_gla"][0].transpose(1, 2, 0, 3),
        "ident": np.eye(P, dtype=np.float32),
        "sel": sel,
        "from_here": (at[:, None] >= at[None]).astype(np.float32), "before": (at[:, None] < at[None]).astype(np.float32),
        "hide_diag": np.where(at[:, None] < at[None], 0, hide).astype(np.float32),
        "hide_self": np.where((s_of[:, None] == q_s[None]) & (t_of[:, None] < q_t[None]), 0, hide).astype(np.float32),
        "causal": np.stack([at[:, None] <= at[None], (at[:, None] <= at[None]) & (s_of[:, None] == s_of[None])], 1).astype(np.float32),
        "goes_on": goes_on,
        "own_rows": (s_of[:, None] == np.arange(SEQS)[None]).astype(np.float32),
        "sixteen": np.tile(np.arange(TOPK, dtype=np.float32), (P, 1)),
    }

def stream_layer_kernel(nc, A, y, kout, vout, prompt_state, sample_state):
    def dram(name, shape):
        return nc.dram_tensor(name, shape, F32, kind="Internal").ap()

    modb = dram("modb", [2, P, MODS])
    oA, oB, mixT = (dram(n, [KC, P, TOK]) for n in ("oA", "oB", "mixT"))
    x1, h2, h2T = dram("x1", [TOK, D]), dram("h2", [TOK, D]), dram("h2T", [TILES, P, D])
    mods_phase(nc, A, modb)
    with nc.sbuf_tensor("hT", [P, KC, TOK], F32) as hT:
        norm_phase(nc, A, modb, hT)
        stick_phase(nc, A, hT, oB, kout, vout)
        gla_phase(nc, A, hT, oA, prompt_state, sample_state)
        mix_phase(nc, A, hT, oA, oB, mixT)
    residual_phase(nc, A, modb, mixT, x1, h2, h2T)
    peer_phase(nc, A, modb, x1, h2, h2T, y)


def kernel(**inputs):
    import numpy as np
    import concourse.bacc as bacc
    from concourse.bass_utils import run_bass_kernel_spmd as run

    nc = bacc.Bacc("TRN2", target_bir_lowering=False, num_devices=1)
    arrays, A = {}, {}
    for name, a in laid_out(inputs).items():
        arrays["in_" + name] = np.ascontiguousarray(a)
        A[name] = nc.dram_tensor("in_" + name, a.shape, mybir.dt.from_np(a.dtype), kind="ExternalInput").ap()
    shapes = {"y": [TOK, D], "k": [TOK, D], "v": [TOK, D], "prompt_state": [GLA_HEADS, DK, DV], "sample_state": [GLA_HEADS, DK, SEQS, DV]}
    outs = [nc.dram_tensor("out_" + name, shape, F32, kind="ExternalOutput").ap() for name, shape in shapes.items()]
    stream_layer_kernel(nc, A, *outs)
    got = run(nc, [arrays], core_ids=[0]).results[0]
    y, k, v, prompt_state, sample_state = (got["out_" + name] for name in shapes)
    heads = (2 * SB_PAIRS, HD)
    return (y[:PROMPT].reshape(1, PROMPT, D), y[PROMPT:].reshape(SEQS, NEW, D),
            prompt_state[None, None], k[:PROMPT].reshape(1, 1, PROMPT, *heads), v[:PROMPT].reshape(1, 1, PROMPT, *heads),
            sample_state.transpose(2, 0, 1, 3)[None], k[PROMPT:].reshape(1, SEQS, NEW, *heads), v[PROMPT:].reshape(1, SEQS, NEW, *heads))
```
